# Optimizing a Trainium2 kernel written in Bass

```python
import jax, jax.numpy as jnp
from jax import lax
import numpy as np

D_MODEL = 1024
BATCH = 1
SEQ = 2048
DEPTH = 1
DEC_BATCH = 8
DEC_SEQ = 4
PAST_LEN = 4096
PAGE_SIZE = 128

D_MIX = D_MODEL
D_LRU = D_MIX // 2
N_LRU_BLOCKS = 8
LRU_BLOCK = D_LRU // N_LRU_BLOCKS
LRU_C = 8.0
CONV_A = 4
D_ATT = D_MIX - D_LRU
N_HEADS = 8
HEAD_DIM = D_ATT // N_HEADS
ROT_DIM = HEAD_DIM // 4
ROPE_THETA = 500000.0
DILATED_PATTERNS = ((128, 1), (512, 4), (2048, 16))
MAX_WINDOW = 2048
ATTN_SCALE = HEAD_DIM ** -0.5
NEG_INF = -1e30
D_IN = 2 * D_LRU + 3 * D_ATT
D_FF = 3 * D_MODEL
CONV_F = 3
EPS = 1e-6

kernel_name = 'hymba_rglru_dilated_swa_convffn_step'

def rmsnorm(x, g):
    xf = x.astype(jnp.float32)
    y = xf * lax.rsqrt(jnp.mean(xf * xf, axis=-1, keepdims=True) + EPS)
    return (y * g.astype(jnp.float32)).astype(x.dtype)

def causal_dwconv(x_ext, w, b):
    width = w.shape[0]
    length = x_ext.shape[1] - width + 1
    out = b + x_ext[:, 0:length] * w[0]
    for j in range(1, width):
        out = out + x_ext[:, j:j + length] * w[j]
    return out

def partial_rope(x, pos):
    half = ROT_DIM // 2
    inv_freq = ROPE_THETA ** (-2.0 * jnp.arange(half, dtype=jnp.float32) / ROT_DIM)
    ang = pos[:, None] * inv_freq[None, :]
    cos = jnp.cos(ang)[None, :, None, :]
    sin = jnp.sin(ang)[None, :, None, :]
    xf = x.astype(jnp.float32)
    x1, x2, rest = xf[..., :half], xf[..., half:ROT_DIM], xf[..., ROT_DIM:]
    out = jnp.concatenate([x1 * cos - x2 * sin, x2 * cos + x1 * sin, rest], axis=-1)
    return out.astype(x.dtype)

def block_diag(x, w, b):
    n, l, _ = x.shape
    xb = x.reshape(n, l, N_LRU_BLOCKS, LRU_BLOCK)
    return jnp.einsum('nlgi,gij->nlgj', xb, w).reshape(n, l, D_LRU) + b

def rg_lru(x, h0, w_r, b_r, w_i, b_i, lam):
    r = jax.nn.sigmoid(block_diag(x, w_r, b_r).astype(jnp.float32))
    gi = jax.nn.sigmoid(block_diag(x, w_i, b_i).astype(jnp.float32))
    log_a = -LRU_C * r * jax.nn.softplus(-lam.astype(jnp.float32))
    a = jnp.exp(log_a)
    u = jnp.sqrt(-jnp.expm1(2.0 * log_a)) * (gi * x.astype(jnp.float32))
    u = u.at[:, 0].add(a[:, 0] * h0.astype(jnp.float32))

    def combine(c1, c2):
        a1, b1 = c1
        a2, b2 = c2
        return a1 * a2, a2 * b1 + b2

    _, h = lax.associative_scan(combine, (a, u), axis=1)
    return h

def dilated_attention_banded(q, k, v, window, dilation):
    n, t_len, h, dh = q.shape
    band = window // dilation
    span = band * dilation
    lp = -(-t_len // span) * span
    nb = lp // span
    pad = ((0, 0), (0, lp - t_len), (0, 0), (0, 0))

    def split(x):
        x = jnp.pad(x, pad).reshape(n, lp // dilation, dilation, h, dh).transpose(0, 2, 1, 3, 4)
        return x.reshape(n, dilation, nb, band, h, dh)

    def with_prev(x):
        prev = jnp.pad(x, ((0, 0), (0, 0), (1, 0), (0, 0), (0, 0), (0, 0)))[:, :, :-1]
        return jnp.concatenate([prev, x], axis=3)

    qs = split(q).astype(jnp.float32)
    kb = with_prev(split(k)).astype(jnp.float32)
    vb = with_prev(split(v)).astype(jnp.float32)
    s = jnp.einsum('nrbqhc,nrbkhc->nrbhqk', qs, kb) * ATTN_SCALE
    qi = jnp.arange(band)[:, None]
    kk = jnp.arange(2 * band)[None, :]
    rel = qi + band - kk
    blk = jnp.arange(nb)[:, None, None]
    ok = (rel >= 0) & (rel <= band) & ((blk > 0) | (kk >= band))
    s = jnp.where(ok[None, None, :, None], s, NEG_INF)
    lse = jax.nn.logsumexp(s, axis=-1)
    pr = jnp.exp(s - lse[..., None])
    o = jnp.einsum('nrbhqk,nrbkhc->nrbqhc', pr, vb)
    o = o.reshape(n, dilation, lp // dilation, h, dh).transpose(0, 2, 1, 3, 4).reshape(n, lp, h, dh)[:, :t_len]
    lse = lse.transpose(0, 1, 2, 4, 3).reshape(n, dilation, lp // dilation, h)
    lse = lse.transpose(0, 2, 1, 3).reshape(n, lp, h)[:, :t_len]
    return lse, o

def dilated_attention_gathered(q, kc, vc, n_hist, window, dilation):
    band = window // dilation
    s_len = q.shape[1]
    idx = n_hist + jnp.arange(s_len)[:, None] - dilation * jnp.arange(band + 1)[None, :]
    valid = idx >= 0
    idx = jnp.maximum(idx, 0)
    kg = kc[:, idx].astype(jnp.float32)
    vg = vc[:, idx].astype(jnp.float32)
    s = jnp.einsum('nshc,nskhc->nshk', q.astype(jnp.float32), kg) * ATTN_SCALE
    s = jnp.where(valid[None, :, None, :], s, NEG_INF)
    lse = jax.nn.logsumexp(s, axis=-1)
    pr = jnp.exp(s - lse[..., None])
    o = jnp.einsum('nshk,nskhc->nshc', pr, vg)
    return lse, o

def combine_dilations(parts):
    lse = jnp.stack([p[0] for p in parts], axis=0)
    o = jnp.stack([p[1] for p in parts], axis=0)
    w = jax.nn.softmax(lse, axis=0)
    return jnp.einsum('pnlh,pnlhc->nlhc', w, o)

def attend_prompt(q, k, v):
    return combine_dilations([dilated_attention_banded(q, k, v, w, d) for w, d in DILATED_PATTERNS])

def make_attend_sample(k_hist, v_hist):
    n_hist = k_hist.shape[1]

    def attend(q, k, v):
        kc = jnp.concatenate([k_hist.astype(k.dtype), k], axis=1)
        vc = jnp.concatenate([v_hist.astype(v.dtype), v], axis=1)
        return combine_dilations([dilated_attention_gathered(q, kc, vc, n_hist, w, d) for w, d in DILATED_PATTERNS])

    return attend

def decoder_layer(x, pos, conv_a_hist, lru_h0, ffn_hist, attend, p):
    n, l, _ = x.shape
    h = rmsnorm(x, p['g_mix'])
    z = h @ p['w_in']
    xa, ga, q, k, v = jnp.split(z, [D_LRU, 2 * D_LRU, 2 * D_LRU + D_ATT, 2 * D_LRU + 2 * D_ATT], axis=-1)
    xa_ext = jnp.concatenate([conv_a_hist.astype(x.dtype), xa], axis=1)
    xa_c = causal_dwconv(xa_ext, p['conv_a_w'], p['conv_a_b'])
    hs = rg_lru(xa_c, lru_h0, p['lru_w_r'], p['lru_b_r'], p['lru_w_i'], p['lru_b_i'], p['lru_lambda'])
    ya = hs.astype(x.dtype) * jax.nn.gelu(ga)
    q = partial_rope(q.reshape(n, l, N_HEADS, HEAD_DIM), pos)
    k = partial_rope(k.reshape(n, l, N_HEADS, HEAD_DIM), pos)
    v = v.reshape(n, l, N_HEADS, HEAD_DIM)
    yb = attend(q, k, v).astype(x.dtype).reshape(n, l, D_ATT)
    x = x + jnp.concatenate([ya, yb], axis=-1) @ p['w_out']
    h = rmsnorm(x, p['g_ffn'])
    uf = h @ p['w_ffn_gate']
    uf_ext = jnp.concatenate([ffn_hist.astype(x.dtype), uf], axis=1)
    uc = causal_dwconv(uf_ext, p['conv_f_w'], p['conv_f_b'])
    x = x + (jax.nn.gelu(uc) * (h @ p['w_ffn_up'])) @ p['w_ffn_down']
    new_state = (xa_ext[:, -(CONV_A - 1):], hs[:, -1].astype(x.dtype), k, v, uf_ext[:, -(CONV_F - 1):])
    return x, new_state

def setup_inputs(seed: int = 0) -> dict:
    key = jax.random.key(seed)
    ks = jax.random.split(key, 26)
    f32 = jnp.float32
    win = min(MAX_WINDOW, PAST_LEN)

    def normal(kk, shape, scale):
        return jax.random.normal(kk, shape, f32) * scale

    def gain(kk, shape):
        return 1.0 + 0.02 * jax.random.normal(kk, shape, f32)

    a_c = jax.random.uniform(ks[13], (DEPTH, D_LRU), f32, 0.9, 0.999)
    a_base = a_c ** (1.0 / LRU_C)
    lru_lambda = jnp.log(a_base) - jnp.log1p(-a_base)
    return {
        'x_prompt': normal(ks[0], (BATCH, SEQ, D_MODEL), 1.0),
        'x_sample': normal(ks[1], (DEC_BATCH, DEC_SEQ, D_MODEL), 1.0),
        'state_conv_a': normal(ks[2], (DEPTH, DEC_BATCH, CONV_A - 1, D_LRU), 1.0),
        'state_lru_h': normal(ks[3], (DEPTH, DEC_BATCH, D_LRU), 0.5),
        'cache_win_k': normal(ks[4], (DEPTH, DEC_BATCH, win, N_HEADS, HEAD_DIM), 1.0),
        'cache_win_v': normal(ks[5], (DEPTH, DEC_BATCH, win, N_HEADS, HEAD_DIM), 1.0),
        'state_conv_ffn': normal(ks[6], (DEPTH, DEC_BATCH, CONV_F - 1, D_FF), 1.0),
        'g_mix': gain(ks[7], (DEPTH, D_MODEL)),
        'w_in': normal(ks[8], (DEPTH, D_MODEL, D_IN), D_MODEL ** -0.5),
        'conv_a_w': normal(ks[9], (DEPTH, CONV_A, D_LRU), CONV_A ** -0.5),
        'conv_a_b': normal(ks[10], (DEPTH, D_LRU), 0.01),
        'lru_w_r': normal(ks[11], (DEPTH, N_LRU_BLOCKS, LRU_BLOCK, LRU_BLOCK), LRU_BLOCK ** -0.5),
        'lru_b_r': normal(ks[12], (DEPTH, D_LRU), 0.01),
        'lru_w_i': normal(ks[14], (DEPTH, N_LRU_BLOCKS, LRU_BLOCK, LRU_BLOCK), LRU_BLOCK ** -0.5),
        'lru_b_i': normal(ks[15], (DEPTH, D_LRU), 0.01),
        'lru_lambda': lru_lambda,
        'w_out': normal(ks[16], (DEPTH, D_MIX, D_MODEL), D_MIX ** -0.5),
        'g_ffn': gain(ks[17], (DEPTH, D_MODEL)),
        'w_ffn_gate': normal(ks[18], (DEPTH, D_MODEL, D_FF), D_MODEL ** -0.5),
        'conv_f_w': normal(ks[19], (DEPTH, CONV_F, D_FF), CONV_F ** -0.5),
        'conv_f_b': normal(ks[20], (DEPTH, D_FF), 0.01),
        'w_ffn_up': normal(ks[21], (DEPTH, D_MODEL, D_FF), D_MODEL ** -0.5),
        'w_ffn_down': normal(ks[22], (DEPTH, D_FF, D_MODEL), D_FF ** -0.5),
        'g_final': gain(ks[23], (D_MODEL,)),
    }

def reference(x_prompt, x_sample, state_conv_a, state_lru_h, cache_win_k, cache_win_v, state_conv_ffn,
              g_mix, w_in, conv_a_w, conv_a_b, lru_w_r, lru_b_r, lru_w_i, lru_b_i, lru_lambda, w_out,
              g_ffn, w_ffn_gate, conv_f_w, conv_f_b, w_ffn_up, w_ffn_down, g_final):
    n_p, seq_p, _ = x_prompt.shape
    n_s, seq_s, _ = x_sample.shape
    pos_p = jnp.arange(seq_p, dtype=jnp.float32)
    pos_s = PAST_LEN + jnp.arange(seq_s, dtype=jnp.float32)
    keep_p = min(MAX_WINDOW, seq_p)
    xp, xs = x_prompt, x_sample
    new_p, new_s = [], []
    for layer in range(DEPTH):
        p = {
            'g_mix': g_mix[layer], 'w_in': w_in[layer], 'conv_a_w': conv_a_w[layer], 'conv_a_b': conv_a_b[layer],
            'lru_w_r': lru_w_r[layer], 'lru_b_r': lru_b_r[layer], 'lru_w_i': lru_w_i[layer], 'lru_b_i': lru_b_i[layer],
            'lru_lambda': lru_lambda[layer], 'w_out': w_out[layer], 'g_ffn': g_ffn[layer],
            'w_ffn_gate': w_ffn_gate[layer], 'conv_f_w': conv_f_w[layer], 'conv_f_b': conv_f_b[layer],
            'w_ffn_up': w_ffn_up[layer], 'w_ffn_down': w_ffn_down[layer],
        }
        xp, st_p = decoder_layer(
            xp, pos_p,
            jnp.zeros((n_p, CONV_A - 1, D_LRU), xp.dtype),
            jnp.zeros((n_p, D_LRU), jnp.float32),
            jnp.zeros((n_p, CONV_F - 1, D_FF), xp.dtype),
            attend_prompt, p)
        xs, st_s = decoder_layer(
            xs, pos_s, state_conv_a[layer], state_lru_h[layer], state_conv_ffn[layer],
            make_attend_sample(cache_win_k[layer], cache_win_v[layer]), p)
        new_p.append((st_p[0], st_p[1], st_p[2][:, -keep_p:], st_p[3][:, -keep_p:], st_p[4]))
        new_s.append(st_s)
    y_prompt = rmsnorm(xp, g_final)
    y_sample = rmsnorm(xs, g_final)
    prompt_conv_a = jnp.stack([s[0] for s in new_p], axis=0)
    prompt_lru_h = jnp.stack([s[1] for s in new_p], axis=0)
    prompt_win_k = jnp.stack([s[2] for s in new_p], axis=0)
    prompt_win_v = jnp.stack([s[3] for s in new_p], axis=0)
    prompt_conv_ffn = jnp.stack([s[4] for s in new_p], axis=0)
    sample_conv_a = jnp.stack([s[0] for s in new_s], axis=0)
    sample_lru_h = jnp.stack([s[1] for s in new_s], axis=0)
    sample_win_k = jnp.stack([s[2] for s in new_s], axis=0)
    sample_win_v = jnp.stack([s[3] for s in new_s], axis=0)
    sample_conv_ffn = jnp.stack([s[4] for s in new_s], axis=0)
    return (y_prompt, y_sample, prompt_conv_a, prompt_lru_h, prompt_win_k, prompt_win_v, prompt_conv_ffn,
            sample_conv_a, sample_lru_h, sample_win_k, sample_win_v, sample_conv_ffn)


_drawn_inputs = setup_inputs


def setup_inputs(seed=0):
    import zlib

    import numpy as np

    out = dict(_drawn_inputs(seed))
    spreads = {}
    factors = {'g_mix': 2.856,
     'lru_b_r': 25.67,
     'lru_b_i': 24.93,
     'g_ffn': 2.755,
     'conv_f_b': 8.0,
     'g_final': 8.427}
    for name, (base, spread) in spreads.items():
        noise = np.random.default_rng([zlib.crc32(name.encode()), seed]).standard_normal(out[name].shape)
        drawn = base * np.exp(spread * noise) if base else spread * noise
        out[name] = __import__('jax').numpy.asarray(drawn.astype(out[name].dtype))
    for name, factor in factors.items():
        out[name] = (out[name] * factor).astype(out[name].dtype)
    return out
```

```python
from collections import namedtuple
from contextlib import ExitStack

import numpy as np

import concourse.bass as bass
from concourse import mybir

F32 = mybir.dt.float32
F32R = mybir.dt.float32r
ALU = mybir.AluOpType
ACT = mybir.ActivationFunctionType
AX = mybir.AxisListType

P = 128
D = 1024
KD = D // P
D_LRU = 512
JT = D_LRU // P
FF = 3 * D
FT = FF // P
CONV_A, CONV_F = 4, 3
HA, HF = CONV_A - 1, CONV_F - 1
SEQ, NS, SS = 2048, 8, 4
SMP = NS * SS
TOK = SMP + SEQ
CHUNKS = 5
C = TOK // CHUNKS
VR = C // 4
PAST = 4096
EPS = 1e-6
HD, ROT, HEADS = 64, 16, 8
D_ATT = HEADS * HD
OS = D_ATT + 2 * HEADS
SCALE = HD ** -0.5
NEG = -1e30
PAST_KEYS = 9
LRU_C = 8.0

W_IN, W_OUT, W_FFN, W_DOWN = 20, KD, 2 * FT, KD * 3
T_IN, T_OUT, T_FFN, T_DOWN = 0, W_IN, W_IN + W_OUT, W_IN + W_OUT + W_FFN
AHEAD = 3
RING = 4
STAGE = 2
N_A = CHUNKS * W_IN
N_ALL = N_A + CHUNKS * (W_OUT + W_FFN + W_DOWN)


def build(nc, a, o):
    with ExitStack() as ctx:
        def sb(name, shape, dt=F32, on=ctx):
            return on.enter_context(nc.sbuf_tensor(name, shape, dt))

        def sem(name):
            return ctx.enter_context(nc.semaphore(name))

        stage = [sb(f"stage{i}", [P, KD, P]) for i in range(STAGE)]
        w_hi = [sb(f"w_hi{i}", [P, KD, P], F32R) for i in range(RING)]
        w_lo = [sb(f"w_lo{i}", [P, KD, P], F32R) for i in range(RING)]
        ones = sb("ones", [P, P])
        gains = sb("gains", [P, 3, KD])
        eps = sb("eps", [P, 1])
        ident = sb("ident", [P, P])
        rstd = sb("rstd", [P, C])
        in_ab = ExitStack()
        qT = sb("qT", [P, JT, TOK], on=in_ab)
        kT = sb("kT", [P, JT, TOK], on=in_ab)
        band = sb("band", [P, 2 * P], on=in_ab)
        in_a = ExitStack()
        xT = sb("xT", [P, KD, C], on=in_a)
        h_hi = sb("h_hi", [P, KD, C], F32R, on=in_a)
        h_lo = sb("h_lo", [P, KD, C], F32R, on=in_a)
        xe = [sb(f"xe{j}", [P, HA + C], on=in_a) for j in range(JT)]
        sx = sb("sx", [P, JT, NS, HA + SS], on=in_a)
        gl = [sb(f"gl{i}", [P, C], on=in_a) for i in range(2)]
        xc = [sb(f"xc{i}", [P, C], on=in_a) for i in range(2)]
        xc_hi = sb("xc_hi", [P, C], F32R, on=in_a)
        xc_lo = sb("xc_lo", [P, C], F32R, on=in_a)
        r_ = sb("r_", [P, C], on=in_a)
        gi = sb("gi", [P, C], on=in_a)
        d_ = [sb(f"d{i}", [P, C], on=in_a) for i in range(2)]
        a_ = sb("a_", [P, C], on=in_a)
        raw = [sb(f"raw{i}", [P, C], on=in_a) for i in range(2)]
        v_cols = sb("v_cols", [P, C], on=in_a)
        v_rows = sb("v_rows", [VR, C // VR * P], on=in_a)
        sh = [sb(f"sh{i}", [P, C], on=in_a) for i in range(2)]
        rope = sb("rope", [P, 2, C], on=in_a)
        sq = [sb(f"sq{i}", [P, C], on=in_a) for i in range(2)]
        ssq = sb("ssq", [P, C], on=in_a)
        gw = sb("gw", [P, 2, JT, P], on=in_a)
        gw_hi = sb("gw_hi", [P, 2, JT, P], F32R, on=in_a)
        gw_lo = sb("gw_lo", [P, 2, JT, P], F32R, on=in_a)
        lru_v = sb("lru_v", [P, 4 + CONV_A, JT], on=in_a)
        sp = sb("sp", [P, 8, JT], on=in_a)
        h_car = sb("h_car", [P, JT], on=in_a)
        h0 = sb("h0", [P, JT, NS], on=in_a)
        a5 = sb("a5", [P, NS, SS + 1], on=in_a)
        u5 = sb("u5", [P, NS, SS + 1], on=in_a)
        h5 = sb("h5", [P, NS, SS + 1], on=in_a)
        hs_o = sb("hs_o", [P, JT, NS], on=in_a)
        sx_o = sb("sx_o", [P, JT, NS, HA], on=in_a)
        xe_o = sb("xe_o", [P, JT, HA], on=in_a)
        in_a.close()
        in_p = ExitStack()
        qp = [sb(f"qp{i}", [P, JT, 2, P], on=in_p) for i in range(2)]
        vb = sb("vb", [P, 4, D_ATT], on=in_p)
        pm = [sb(f"pm{i}", [P, 2, 2 * P], on=in_p) for i in range(4)]
        pt = [sb(f"pt{i}", [P, 2, 2, P], on=in_p) for i in range(2)]
        nm = sb("nm", [P, 4, 2], on=in_p)
        st = sb("st", [P, 4, 2, HEADS], on=in_p)
        ob = [sb(f"ob{i}", [P, OS], on=in_p) for i in range(2)]
        oc = [sb(f"oc{i}", [P, 2, OS], on=in_p) for i in range(2)]
        cm = sb("cm", [P, HEADS], on=in_p)
        ce = sb("ce", [P, 3, HEADS], on=in_p)
        cw = sb("cw", [P, 3, HEADS], on=in_p)
        cd = sb("cd", [P, HEADS], on=in_p)
        yt = [sb(f"yt{i}", [P, JT, P], on=in_p) for i in range(2)]
        past = [sb(f"past{i}", [P, 2, PAST_KEYS * P], on=in_p) for i in range(4)]
        smp_q = sb("smp_q", [P, JT, SMP, 2], on=in_p)
        v_new = sb("v_new", [SMP, D_ATT], on=in_p)
        past_mask = sb("past_mask", [P, 3 * P], on=in_p)
        new_mask = sb("new_mask", [P, 2, 3, SMP], on=in_p)
        turned_s = sb("turned_s", [P, 4 * P], on=in_p)
        smp_p = sb("smp_p", [P, 3 * P + 3 * SMP], on=in_p)
        smp_m = sb("smp_m", [P, 4], on=in_p)
        smp_y = sb("smp_y", [P, JT, SMP // 2], on=in_p)
        in_p.close()
        in_ab.close()
        in_c = ExitStack()
        cf = sb("cf", [P, 1 + CONV_F, FT], on=in_c)
        x1 = sb("x1", [P, KD, C], on=in_c)
        res = sb("res", [P, KD, C], on=in_c)
        hb_hi = sb("hb_hi", [P, KD, C], F32R, on=in_c)
        hb_lo = sb("hb_lo", [P, KD, C], F32R, on=in_c)
        ff_hi = sb("ff_hi", [P, FT, C], F32R, on=in_c)
        ff_lo = sb("ff_lo", [P, FT, C], F32R, on=in_c)
        xs = [sb(f"xs{i}", [P, C], on=in_c) for i in range(2)]
        gx = [sb(f"gx{i}", [P, HF + C], on=in_c) for i in range(2)]
        gs = [sb(f"gs{i}", [P, NS, HF + SS], on=in_c) for i in range(2)]
        uc = [sb(f"uc{i}", [P, C], on=in_c) for i in range(2)]
        sf = sb("sf", [P, FT, NS, HF], on=in_c)
        carry = sb("carry", [P, FT, HF], on=in_c)
        sqf = [sb(f"sqf{i}", [P, C], on=in_c) for i in range(2)]
        ssf = sb("ssf", [P, C], on=in_c)
        in_c.close()

        bank = [ctx.enter_context(nc.psum_tensor(f"bank{i}", [P, 512], F32)) for i in range(8)]

        w_loaded = [sem(f"w_loaded{i}") for i in range(STAGE)]
        hi_ready, lo_ready = sem("hi_ready"), sem("lo_ready")
        tile_done = sem("tile_done")
        evacuated = [sem(f"evacuated{i}") for i in range(4)]
        par_loaded, par_ready = sem("par_loaded"), sem("par_ready")
        gw_zeroed, gw_loaded, gw_split, gw_ready = sem("gw_zeroed"), sem("gw_loaded"), sem("gw_split"), sem("gw_ready")
        sp_step, log1p_step = sem("sp_step"), sem("log1p_step")
        xt_loaded, sq_step, ms_ready, rms_ready, rstd_ready = (sem(x) for x in ("xt_loaded", "sq_step", "ms_ready", "rms_ready", "rstd_ready"))
        hn_ready, hh_ready, hl_ready = sem("hn_ready"), sem("hh_ready"), sem("hl_ready")
        xa_carried, tap0_done, taps, smp_tap = sem("xa_carried"), sem("tap0_done"), sem("taps"), sem("smp_tap")
        xch_ready, xcl_ready, gates_done, r_ready, gi_ready, t_ready = (sem(x) for x in ("xch_ready", "xcl_ready", "gates_done", "r_ready", "gi_ready", "t_ready"))
        d1_ready, d_ready, s_ready, lru_a, u1_ready, sd_ready, u_ready, h_ready, h_carried, ya_ready = (sem(x) for x in (
            "d1_ready", "d_ready", "s_ready", "lru_a", "u1_ready", "sd_ready", "u_ready", "h_ready", "h_carried", "ya_ready"))
        ya_stored = [sem(f"ya_stored{i}") for i in range(2)]
        smp_step, smp_copied = sem("smp_step"), sem("smp_copied")
        rope_loaded, shuffled, sin_done, roped = (sem(x) for x in ("rope_loaded", "shuffled", "sin_done", "roped"))
        v_stored, v_turned, v_ready = sem("v_stored"), sem("v_turned"), sem("v_ready")
        made, ident_ready, band_ready = sem("made"), sem("ident_ready"), sem("band_ready")
        (a_done, qp_zeroed, q_copied, qk_done, maxed, masked, exp_done, tr_done, pt_ready, pv_done, o_out) = (sem(x) for x in (
            "a_done", "qp_zeroed", "q_copied", "qk_done", "maxed", "masked", "exp_done", "tr_done", "pt_ready", "pv_done", "o_out"))
        vb_loaded = [sem(f"vb_loaded{i}") for i in range(4)]
        os_stored = [sem(f"os_stored{i}") for i in range(2)]
        oc_loaded = [sem(f"oc_loaded{i}") for i in range(2)]
        cm_max, cm_step, cm_exp, cm_rec, cm_dve, y_turned, yt_ready = (
            sem(x) for x in ("cm_max", "cm_step", "cm_exp", "cm_rec", "cm_dve", "y_turned", "yt_ready"))
        yt_stored = [sem(f"yt_stored{i}") for i in range(2)]
        past_loaded = [sem(f"past_loaded{i}") for i in range(4)]
        smp_loaded, smp_q_ready, past_used, new_scored, st_copied, st_turned, sm_step, sm_exp, p_turned, pt_copied, smp_y_ready, smp_stored = (
            sem(x) for x in ("smp_loaded", "smp_q_ready", "past_used", "new_scored", "st_copied", "st_turned", "sm_step",
                             "sm_exp", "p_turned", "pt_copied", "smp_y_ready", "smp_stored"))
        sp_passed, dve_passed, pool_passed = sem("sp_passed"), sem("dve_passed"), sem("pool_passed")
        c_free, cf_loaded, y_loaded = sem("c_free"), sem("cf_loaded"), sem("y_loaded")
        hbh_ready, hbl_ready, res_copied = sem("hbh_ready"), sem("hbl_ready"), sem("res_copied")
        xs_loaded = [sem(f"xs_loaded{i}") for i in range(2)]
        halo_ready, carried, ftap0, ftaps, stap, gelu_done, ffh_ready, ffl_ready = (sem(x) for x in (
            "halo_ready", "carried", "ftap0", "ftaps", "stap", "gelu_done", "ffh_ready", "ffl_ready"))
        fsq_step, fms_ready, frms_ready, frstd_ready, fhn_ready, final_ready, final_stored, zeroed = (sem(x) for x in (
            "fsq_step", "fms_ready", "frms_ready", "frstd_ready", "fhn_ready", "final_ready", "final_stored", "zeroed"))
        final_last = sem("final_last")
        k_stored, stored = sem("k_stored"), sem("stored")

        block = ctx.enter_context(nc.Block())

        def chunks(e, body):
            body(0, True, True)
            with e.Fori(1, CHUNKS - 1) as c:
                body(c, False, True)
            body(CHUNKS - 1, False, False)

        def cols(c):
            return bass.ds(c * C, C)

        def blk(order, k, n):
            i = 4 * k + n
            dil = (4, 16, 1)[order]
            first = SMP + (k + 4 * P * n if order == 0 else i if order == 1 else P * i)
            prev = (n > 0, False, not (isinstance(i, int) and i == 0))[order]
            return Block(order, 16 * order + i, 4 * order + k, k, n, first, dil, prev)

        def attention(e, body):
            def turn(order, k, then, unit=None):
                for n in range(4):
                    body(blk(order, k, n), blk(order, k, n + 1) if n < 3 else then, unit)

            for k in range(4):
                turn(0, k, blk(0, k + 1, 0) if k < 3 else blk(1, 0, 0), "keys" if k < 2 else "values")
            with e.Fori(0, 2) as k:
                turn(1, k, blk(1, k + 1, 0), "keys")
            turn(1, 2, blk(1, 3, 0), "values")
            turn(1, 3, blk(2, 0, 0), "values")
            turn(2, 0, blk(2, 1, 0))
            with e.Fori(1, 3) as k:
                turn(2, k, blk(2, k + 1, 0))
            turn(2, 3, None)

        def ahead_by(cur, nxt, t, lag):
            return (cur, t + lag) if t + lag < 4 else (nxt, t + lag - 4)

        def tile_c(c, t):
            return N_A + W_OUT + (W_FFN + W_OUT + W_DOWN) * c + t

        def tile_out(c):
            return N_A if isinstance(c, int) and c == 0 else tile_c(c - 1, W_FFN)

        EV_C = (N_A + W_OUT) // 4
        EV_CHUNK = (W_FFN + W_OUT + KD) // 4

        def ev_ffn(c):
            return EV_C + EV_CHUNK * c

        def ev_out(c):
            return N_A // 4 if isinstance(c, int) and c == 0 else ev_ffn(c - 1) + W_FFN // 4

        def ev_down(c, more):
            return ev_ffn(c) + (W_FFN + (W_OUT if more else 0)) // 4

        def norm_in(c):
            return 0 if isinstance(c, int) and c == 0 else 2 * c - 1

        def norm_out(c, more):
            return 2 * c + 2 if more else 2 * c + 1

        @block.sync
        def _(e):
            def load_tile(n, s, t):
                if not (isinstance(n, int) and n < STAGE):
                    e.wait_ge(lo_ready, n - STAGE + 1)
                e.dma_start(stage[s][:], a["w"][bass.ds(t, 1)].rearrange("a p k n -> (a p) k n")).then_inc(w_loaded[s], 16)

            e.dma_start(xT[:], a["x"][:, :, 0:C]).then_inc(xt_loaded, 16)
            e.dma_start(gains[:], a["gains"]).then_inc(par_loaded, 16)
            e.dma_start(lru_v[:], a["lru_v"]).then_inc(par_loaded, 16)
            e.dma_start(sx[:, :, :, 0:HA], a["state_a"]).then_inc(par_loaded, 16)
            e.dma_start(h0[:], a["h0"]).then_inc(par_loaded, 16)
            e.wait_ge(gw_zeroed, 1)
            for g in range(2):
                for half in range(2):
                    q = slice(64 * half, 64 * half + 64)
                    e.dma_start(gw[q, g, :, q], a["gates_w"][g, half]).then_inc(gw_loaded, 16)

            def chunk(c, first, more):
                for t in range(W_IN):
                    load_tile(c * W_IN + t, t % STAGE, T_IN + t)

            def passed():
                e.sem_inc(sp_passed, 1)

            def load_v(b):
                e.dma_start(vb[:, b.n], o["v"][bass.ds(b.first, P, b.dil), :]).then_inc(vb_loaded[b.n], 16)

            def load_past(u, slot):
                e.dma_start(past[slot][:], a["past"][bass.ds(u, 1)].rearrange("a p t k -> (a p) t k")).then_inc(past_loaded[slot], 16)

            def attention_loads():
                e.wait_ge(a_done, 1)
                load_v(blk(0, 0, 0))
                load_past(0, 0)
                e.dma_start(v_new[:], o["v"][0:SMP, :]).then_inc(smp_loaded, 16)
                e.dma_start(past_mask[:], a["past_mask"]).then_inc(smp_loaded, 16)
                e.dma_start(new_mask[:], a["new_mask"]).then_inc(smp_loaded, 16)
                load_past(1, 1)
                load_past(2, 2)

                def body(cur, nxt, unit):
                    par = cur.n % 2
                    if nxt:
                        e.wait_ge(pv_done, 4 * cur.idx)
                        passed()
                        load_v(nxt)
                    if unit and not (isinstance(cur.idx, int) and cur.idx > 28):
                        if not (isinstance(cur.idx, int) and cur.idx == 0):
                            e.wait_ge(past_used, cur.idx)
                        passed()
                        load_past(cur.idx + 3, (cur.n + 3) % 4)
                    if cur.order < 2:
                        e.wait_ge(o_out, cur.idx + 1)
                        passed()
                        e.dma_start(a["os"][cur.order, bass.ds(cur.first - SMP, P, cur.dil), :], ob[par][:]).then_inc(os_stored[par], 16)
                    else:
                        y = cur.idx - 32
                        if isinstance(y, int) and y == 0:
                            for s in range(2):
                                e.wait_ge(os_stored[s], 16 * 16)
                        if not (isinstance(y, int) and y < 2):
                            e.wait_ge(cm_dve, 3 * (y - 1))
                        passed()
                        e.dma_start(oc[par][:], a["os"][:, bass.ds(cur.first - SMP, P), :].rearrange("o p n -> p o n")).then_inc(oc_loaded[par], 16)

                attention(e, body)

            chunks(e, chunk)
            for d in range(AHEAD + STAGE):
                load_tile(N_A + d, d % STAGE, T_OUT + d)
            e.wait_ge(smp_copied, 2)
            e.dma_start(o["s_conv_a"], sx_o[:]).then_inc(stored, 16)
            e.wait_ge(smp_step, 6 * JT)
            e.dma_start(o["s_lru_h"], hs_o[:]).then_inc(stored, 16)
            e.wait_ge(smp_copied, 3)
            e.dma_start(o["p_conv_a"], xe_o[:]).then_inc(stored, 16)
            e.wait_ge(h_carried, JT * CHUNKS)
            e.dma_start(o["p_lru_h"], h_car[:]).then_inc(stored, 16)
            e.wait_ge(k_stored, 16 * CHUNKS)
            e.wait_ge(v_stored, 16 * JT * CHUNKS)
            attention_loads()
            for s in range(2):
                e.wait_ge(ya_stored[s], 16 * 2 * CHUNKS)
                e.wait_ge(yt_stored[s], 16 * 8)

            def load_y(c):
                e.dma_start(x1[:, 0:JT], a["ya"][:, :, cols(c)]).then_inc(y_loaded, 16)
                e.dma_start(x1[:, JT:], a["yb"][:, :, cols(c)]).then_inc(y_loaded, 16)

            e.wait_ge(c_free, 1)
            e.wait_ge(smp_stored, 32)
            load_y(0)
            e.dma_start(cf[:], a["conv_f"]).then_inc(cf_loaded, 16)
            e.dma_start(sf[:], a["state_f"]).then_inc(cf_loaded, 16)
            for d in range(AHEAD + STAGE, W_OUT):
                load_tile(N_A + d, d % STAGE, T_OUT + d)

            def ffn_chunk(c, first, more):
                for t in range(W_FFN):
                    load_tile(tile_c(c, t), t % STAGE, T_FFN + t)
                    if t == 44 and more:
                        e.wait_ge(res_copied, KD * (c + 1))
                        passed()
                        load_y(c + 1)
                for d in range(W_OUT if more else 0):
                    load_tile(tile_c(c, W_FFN + d), d % STAGE, T_OUT + d)
                for s in range(W_DOWN):
                    load_tile(tile_c(c, W_FFN + (W_OUT if more else 0) + s), s % STAGE, T_DOWN + s)

            chunks(e, ffn_chunk)
            e.wait_ge(carried, FT * CHUNKS)
            e.dma_start(o["p_conv_f"], carry[:]).then_inc(stored, 16)
            e.dma_start(o["s_conv_f"], sf[:]).then_inc(stored, 16)
            e.wait_ge(stored, 16 * 6)
            e.wait_ge(final_stored, 16 * (CHUNKS - 1))

        @block.scalar
        def _(e):
            def split_hi(n, s):
                e.wait_ge(w_loaded[s % STAGE], 16 * (n // STAGE) + 16 if isinstance(n, int) else 8 * (n - s % STAGE) + 16)
                if not (isinstance(n, int) and n < RING):
                    e.wait_ge(tile_done, n - RING + 1)
                e.activation(w_hi[s][:], stage[s % STAGE][:], ACT.Copy).then_inc(hi_ready, 1)

            e.wait_ge(xt_loaded, 16)
            for n in range(AHEAD):
                split_hi(n, n)
            e.wait_ge(gw_loaded, 64)
            e.activation(gw_hi[:], gw[:], ACT.Copy).then_inc(gw_split, 1)
            e.wait_ge(par_loaded, 64)
            e.activation(sp[:, 1], lru_v[:, 2], ACT.Abs).then_inc(sp_step, 1)
            e.wait_ge(sp_step, 1)
            e.activation(sp[:, 2], sp[:, 1], ACT.Exp, scale=-1.0).then_inc(sp_step, 1)
            e.wait_ge(ms_ready, 1)
            e.wait_ge(par_ready, 1)
            e.activation(rstd[:], bank[4][:, 0:C], ACT.Sqrt, bias=eps[:, 0:1]).then_inc(rms_ready, 1)

            def done(c, t):
                e.wait_ge(tile_done, c * W_IN + t + 1)
                return bank[t % 4]

            def store_v(m, c, j):
                e.wait_ge(v_turned, m + 1)
                if not (isinstance(m, int) and m == 0):
                    e.wait_ge(v_stored, 16 * m)
                e.activation(v_rows[:], bank[7][0:VR, :], ACT.Copy).then_inc(v_ready, 1)
                e.wait_ge(v_ready, m + 1)
                e.dma_start(o["v"][cols(c), j * P:(j + 1) * P].rearrange("(b i) n -> i b n", i=VR),
                            v_rows[:].rearrange("i (b n) -> i b n", n=P)).then_inc(v_stored, 16)

            def ahead(c, t, more):
                split_hi(c * W_IN + t + AHEAD, (t + AHEAD) % RING)

            def chunk(c, first, more):
                if not first:
                    e.wait_ge(tile_done, c * W_IN)
                for k in range(KD):
                    e.wait_ge(hn_ready, KD * c + k + 1)
                    e.activation(h_hi[:, k], xT[:, k], ACT.Copy).then_inc(hh_ready, 1)
                for j in range(JT):
                    m = JT * c + j
                    lo = SMP if first else 0
                    x_a, g_a, qk, v_t = 5 * j, 5 * j + 1, (5 * j + 2, 5 * j + 3), 5 * j + 4
                    ahead(c, x_a, more)
                    if not first:
                        e.wait_ge(taps, 3 * (m - JT) + 3)
                        e.activation(xe[j][:, 0:HA], xe[j][:, C:C + HA], ACT.Copy).then_inc(xa_carried, 1)
                        e.wait_ge(xa_carried, m - JT + 1)
                    elif j == 0:
                        e.wait_ge(par_ready, 1)
                    b = done(c, x_a)
                    if first:
                        e.activation(sx[:, j, :, HA:], b[:, 0:SMP].rearrange("p (n s) -> p n s", s=SS), ACT.Copy)
                    e.activation(xe[j][:, HA + lo:], b[:, lo:C], ACT.Copy).then_inc(evacuated[x_a % 4], 1)
                    e.wait_ge(evacuated[x_a % 4], 5 * c + x_a // 4 + 1)
                    if not (first and j < 2):
                        e.wait_ge(u1_ready, m - 1)
                    if first:
                        e.activation(xc[j % 2][:, 0:SMP].rearrange("p (n s) -> p n s", s=SS), sx[:, j, :, 0:SS], ACT.Identity,
                                     bias=lru_v[:, 3, j:j + 1], scale=lru_v[:, 4, j:j + 1])
                    e.activation(xc[j % 2][:, lo:], xe[j][:, lo:C], ACT.Identity,
                                 bias=lru_v[:, 3, j:j + 1], scale=lru_v[:, 4, j:j + 1]).then_inc(tap0_done, 1)
                    if j == 0 and more:
                        e.wait_ge(hl_ready, KD * (c + 1))
                        e.dma_start(xT[:], a["x"][:, :, cols(c + 1)]).then_inc(xt_loaded, 16)
                    if j == 0:
                        if not first:
                            e.wait_ge(roped, 8 * c)
                        e.dma_start(rope[:], a["rope"][:, :, cols(c)]).then_inc(rope_loaded, 16)
                    if not (first and j == 0):
                        store_v(m - 1, c if j else c - 1, (j - 1) % JT)
                    ahead(c, g_a, more)
                    e.wait_ge(taps, 3 * m + 3)
                    if first:
                        e.wait_ge(smp_tap, 3 * m + 3)
                    if not (first and j == 0):
                        e.wait_ge(gates_done, m)
                    e.activation(xc_hi[:], xc[j % 2][:], ACT.Copy).then_inc(xch_ready, 1)
                    b = done(c, g_a)
                    if not (first and j < 2):
                        e.wait_ge(ya_ready, m - 1)
                    e.activation(gl[j % 2][:], b[:, 0:C], ACT.Gelu_apprx_tanh).then_inc(evacuated[g_a % 4], 1)
                    for i, t in enumerate(qk):
                        ahead(c, t, more)
                        if i == 1:
                            e.wait_ge(gates_done, m + 1)
                            if not (first and j == 0):
                                e.wait_ge(h_carried, m)
                                e.wait_ge(ya_ready, m)
                            e.activation(r_[:], bank[5][:, 0:C], ACT.Sigmoid, bias=lru_v[:, 0, j:j + 1]).then_inc(r_ready, 1)
                            e.activation(gi[:], bank[6][:, 0:C], ACT.Sigmoid, bias=lru_v[:, 1, j:j + 1]).then_inc(gi_ready, 1)
                            e.wait_ge(r_ready, m + 1)
                            if first and j == 0:
                                e.wait_ge(sp_step, 13)
                            e.activation(r_[:], r_[:], ACT.Tanh, scale=sp[:, 0, j:j + 1]).then_inc(t_ready, 1)
                        b = done(c, t)
                        if not (first and j == 0):
                            e.wait_ge(shuffled, 2 * m + i - 1)
                        e.activation(raw[i][:], b[:, 0:C], ACT.Copy).then_inc(evacuated[t % 4], 1)
                    ahead(c, v_t, more)
                    e.wait_ge(d1_ready, m + 1)
                    e.activation(r_[:], r_[:], ACT.Sqrt, scale=4.0).then_inc(s_ready, 1)
                    if j == 2 and more:
                        e.wait_ge(ms_ready, c + 2)
                        e.wait_ge(hn_ready, KD * (c + 1))
                        e.activation(rstd[:], bank[4][:, 0:C], ACT.Sqrt, bias=eps[:, 0:1]).then_inc(rms_ready, 1)
                    b = done(c, v_t)
                    if not (first and j == 0):
                        e.wait_ge(v_turned, m)
                    e.activation(v_cols[:], b[:, 0:C], ACT.Copy).then_inc(evacuated[v_t % 4], 1)

            chunks(e, chunk)
            store_v(JT * CHUNKS - 1, CHUNKS - 1, JT - 1)

            def exps(b, t):
                e.wait_ge(masked, 4 * b.idx + t + 1)
                for hd in range(2):
                    v = pm[t][:, hd, (0 if b.prev else P):]
                    ins = e.activation(v, v, ACT.Exp, bias=nm[:, t, hd:hd + 1], scale=SCALE,
                                       accum_out=st[:, b.n, 1, 2 * t + hd:2 * t + hd + 1])
                ins.then_inc(exp_done, 1)

            def turned(b, t):
                u = 4 * b.idx + t
                e.wait_ge(tr_done, u + 1)
                if not (isinstance(u, int) and u < 2):
                    e.wait_ge(pv_done, u - 1)
                k0 = 0 if b.prev else 1
                e.activation(pt[t % 2][:, :, k0:], bank[4 + t % 2][:].rearrange("p (h k q) -> p h k q", h=2, k=2)[:, :, k0:],
                             ACT.Copy).then_inc(pt_ready, 1)

            def y_out(y, par):
                e.wait_ge(y_turned, y + 1)
                if not (isinstance(y, int) and y < 2):
                    e.wait_ge(yt_stored[par], 8 * (y - par))
                e.activation(yt[par][:], bank[7][:].rearrange("p (j q) -> p j q", q=P), ACT.Copy).then_inc(yt_ready, 1)
                e.wait_ge(yt_ready, y + 1)
                e.dma_start(a["yb"][:, :, bass.ds(SMP + P * y, P)], yt[par][:]).then_inc(yt_stored[par], 16)

            def combine_exp(y):
                e.wait_ge(cm_step, 11 * y + 3)
                e.activation(ce[:], ce[:], ACT.Exp, scale=SCALE).then_inc(cm_exp, 1)

            def body(cur, nxt, unit):
                y = cur.idx - 32
                for t in range(4):
                    b, i = ahead_by(cur, nxt, t, 2)
                    if b:
                        exps(b, i)
                    b, i = ahead_by(cur, nxt, t, 1)
                    if b:
                        turned(b, i)
                    if unit == "values" and cur.idx % 16 == 8:
                        sample_step(cur.order, t)
                    if cur.order == 2 and not (isinstance(y, int) and y < 1) and t == 0:
                        combine_exp(y - 1)
                    if cur.order == 2 and not (isinstance(y, int) and y < 2) and t == 1:
                        y_out(y - 2, cur.n % 2)
                if unit == "values" and cur.idx % 16 == 15:
                    sample_out(cur.order)

            def turned_out(done, count, copied):
                e.wait_ge(done, count)
                e.activation(turned_s[:, 0:3 * P], bank[7][:, 0:3 * P], ACT.Copy)
                e.activation(turned_s[0:SMP, 3 * P:], bank[7][0:SMP, 3 * P:], ACT.Copy).then_inc(copied, 1)

            def sample_step(g, t):
                if t == 0:
                    turned_out(new_scored, g + 1, st_copied)
                if t == 2:
                    e.wait_ge(sm_step, 8 * g + 4)
                    e.activation(smp_p[:], smp_p[:], ACT.Exp, bias=smp_m[:, 2:3], scale=SCALE, accum_out=smp_m[:, 3:4]).then_inc(sm_exp, 1)
                if t == 3:
                    turned_out(p_turned, g + 1, pt_copied)

            def sample_out(g):
                e.wait_ge(past_used, 16 * (g + 1))
                if g:
                    e.wait_ge(smp_stored, 16 * g)
                for hd in range(2):
                    rows = slice(HD * hd, HD * hd + HD)
                    ins = e.activation(smp_y[rows], bank[7][rows, 0:P].rearrange("p (t k d) -> p t k d", t=JT, d=2)[:, :, :, hd], ACT.Copy)
                ins.then_inc(smp_y_ready, 1)
                e.wait_ge(smp_y_ready, g + 1)
                e.dma_start(a["yb"][:, :, SMP // 2 * g:SMP // 2 * (g + 1)], smp_y[:]).then_inc(smp_stored, 16)

            exps(blk(0, 0, 0), 0)
            exps(blk(0, 0, 0), 1)
            turned(blk(0, 0, 0), 0)
            attention(e, body)
            combine_exp(15)
            y_out(14, 0)
            y_out(15, 1)

            def ahead_c(n, t):
                split_hi(n + t + AHEAD, (t + AHEAD) % RING)

            def part_hi(g, k, src):
                e.activation(hb_hi[:, k], src, ACT.Copy).then_inc(hbh_ready, 1)

            def load_x(c, d):
                e.dma_start(xs[d % 2][:], a["x"][:, d, cols(c)]).then_inc(xs_loaded[d % 2], 16)

            def root(q):
                e.wait_ge(fms_ready, q + 1)
                e.activation(rstd[:], bank[4][:, 0:C], ACT.Sqrt, bias=eps[:, 0:1]).then_inc(frms_ready, 1)

            def heads_product(c, last):
                e.wait_ge(tile_done, tile_out(c))
                for k in range(KD):
                    if k == 0:
                        e.wait_ge(y_loaded, 32 * c + 32)
                    part_hi(2 * c, k, x1[:, k])
                for d in range(W_OUT):
                    ahead_c(tile_out(c), d)
                    if d >= 1 and d + 1 < W_OUT:
                        e.wait_ge(evacuated[(d - 1) % 4], ev_out(c) + (d - 1) // 4 + 1)
                        load_x(c, d + 1)

            def store_out(c):
                e.wait_ge(final_ready, KD * (c + 1))
                e.dma_start(o["y"][:, :, cols(c)], res[:]).then_inc(final_stored, 16)

            def normed_hi(c, k):
                e.wait_ge(fhn_ready, KD * c + k + 1)
                part_hi(2 * c + 1, k, uc[k % 2][:])

            def ffn_chunk(c, first, more):
                n = tile_c(c, 0)
                for t in range(W_FFN):
                    f = t // 2
                    F = FT * c + f
                    u = f % 2
                    lo = SMP if first else 0
                    ahead_c(n, t)
                    if t == 2 and not first:
                        e.wait_ge(fhn_ready, KD * (c + 1))
                        root(2 * c)
                    if t == 12 and not first:
                        store_out(c - 1)
                    if t == 44 and more:
                        e.wait_ge(evacuated[2], ev_ffn(c))
                        e.wait_ge(evacuated[3], ev_ffn(c))
                        load_x(c + 1, 0)
                        load_x(c + 1, 1)
                    if t % 2 == 0:
                        if f > 0:
                            e.wait_ge(evacuated[(t - 1) % 4], ev_ffn(c) + (t - 1) // 4 + 1)
                            e.activation(ff_hi[:, f - 1], uc[1 - u][:], ACT.Copy).then_inc(ffh_ready, 1)
                        e.wait_ge(tile_done, n + t + 1)
                        if not (first and f < 2):
                            e.wait_ge(ftaps, 2 * F - 2)
                            e.wait_ge(carried, F - 1)
                        b = bank[t % 4]
                        if first:
                            e.activation(gs[u][:, :, HF:], b[:, 0:SMP].rearrange("p (n s) -> p n s", s=SS), ACT.Copy)
                        e.activation(gx[u][:, HF + lo:], b[:, lo:C], ACT.Copy).then_inc(evacuated[t % 4], 1)
                        e.wait_ge(evacuated[t % 4], ev_ffn(c) + t // 4 + 1)
                        e.wait_ge(halo_ready, F + 1)
                        if not (first and f < 2):
                            e.wait_ge(ffl_ready, F - 1)
                        if first:
                            e.activation(uc[u][:, 0:SMP].rearrange("p (n s) -> p n s", s=SS), gs[u][:, :, 0:SS], ACT.Identity,
                                         bias=cf[:, 0, f:f + 1], scale=cf[:, 1, f:f + 1])
                        e.activation(uc[u][:, lo:], gx[u][:, lo:C], ACT.Identity,
                                     bias=cf[:, 0, f:f + 1], scale=cf[:, 1, f:f + 1]).then_inc(ftap0, 1)
                    else:
                        e.wait_ge(ftaps, 2 * F + 2)
                        if first:
                            e.wait_ge(stap, 2 * F + 2)
                        e.activation(uc[u][:], uc[u][:], ACT.Gelu_apprx_tanh).then_inc(gelu_done, 1)
                e.wait_ge(evacuated[3], ev_ffn(c) + W_FFN // 4)
                e.activation(ff_hi[:, FT - 1], uc[1][:], ACT.Copy).then_inc(ffh_ready, 1)
                if more:
                    heads_product(c + 1, False)
                n = tile_c(c, W_FFN + (W_OUT if more else 0))
                for s in range(W_DOWN):
                    if more or s < W_DOWN - AHEAD:
                        ahead_c(n, s)
                    if more and s == 2:
                        root(norm_in(c + 1))
                    if more and 4 <= s < 4 + KD:
                        normed_hi(c + 1, s - 4)

            e.wait_ge(c_free, 1)
            load_x(0, 0)
            load_x(0, 1)
            heads_product(0, False)
            root(0)
            for k in range(KD):
                normed_hi(0, k)
            e.wait_ge(cf_loaded, 32)
            chunks(e, ffn_chunk)
            root(norm_out(CHUNKS - 1, False))
            for k in range(KD):
                e.wait_ge(final_ready, KD * (CHUNKS - 1) + k + 1)
                e.dma_start(o["y"][:, k, cols(CHUNKS - 1)], res[:, k]).then_inc(final_last, 16)
            e.wait_ge(final_last, 16 * KD)

        @block.vector
        def _(e):
            e.memset(gw[:], 0.0).then_inc(gw_zeroed, 1)
            e.memset(ones[:], 1.0 / D)
            for j in range(JT):
                e.memset(xe[j][:, 0:HA + SMP], 0.0)
            e.memset(a5[:], 0.0)
            e.memset(eps[:], EPS).then_inc(par_ready, 1)

            def split_lo(n, s):
                e.wait_ge(hi_ready, n + 1)
                e.tensor_tensor(w_lo[s][:], stage[s % STAGE][:], w_hi[s][:].bitcast(F32), ALU.subtract).then_inc(lo_ready, 1)

            def ahead(c, t, more):
                split_lo(c * W_IN + t + AHEAD, (t + AHEAD) % RING)

            def norm_scale(c, ks):
                for k in ks:
                    e.scalar_tensor_tensor(out=xT[:, k], in0=xT[:, k], scalar=gains[:, 0, k:k + 1], in1=rstd[:],
                                           op0=ALU.mult, op1=ALU.mult).then_inc(hn_ready, 1)

            for n in range(AHEAD):
                split_lo(n, n)
            e.wait_ge(rms_ready, 1)
            e.wait_ge(par_loaded, 64)
            e.reciprocal(rstd[:], rstd[:]).then_inc(rstd_ready, 1)
            e.wait_ge(rstd_ready, 1)
            norm_scale(0, range(KD))
            e.wait_ge(gw_split, 1)
            e.tensor_tensor(gw_lo[:], gw[:], gw_hi[:].bitcast(F32), ALU.subtract).then_inc(gw_ready, 1)

            def softplus():
                x, s, s2, acc = sp[:, 2], sp[:, 3], sp[:, 4], sp[:, 5]
                count = [2]

                def step(ins):
                    ins.then_inc(sp_step, 1)
                    count[0] += 1
                    e.wait_ge(sp_step, count[0])

                e.wait_ge(sp_step, 2)
                step(e.tensor_scalar(s, x, 2.0, None, ALU.add))
                step(e.reciprocal(s, s))
                step(e.tensor_tensor(s, s, x, ALU.mult))
                step(e.tensor_tensor(s2, s, s, ALU.mult))
                step(e.memset(acc, 1.0 / 17))
                for k in range(15, 0, -2):
                    e.tensor_tensor(acc, acc, s2, ALU.mult).then_inc(series, 1)
                    count[0] += 0
                    ser[0] += 1
                    e.wait_ge(series, ser[0])
                    e.tensor_scalar(acc, acc, 1.0 / k, None, ALU.add).then_inc(series, 1)
                    ser[0] += 1
                    e.wait_ge(series, ser[0])
                step(e.tensor_tensor(acc, acc, s, ALU.mult))
                step(e.tensor_scalar(sp[:, 6], lru_v[:, 2], -1.0, 0.0, ALU.mult, ALU.max))
                step(e.tensor_scalar(acc, acc, LRU_C, None, ALU.mult))
                step(e.tensor_scalar(sp[:, 6], sp[:, 6], LRU_C / 2, None, ALU.mult))
                step(e.tensor_tensor(sp[:, 7], acc, sp[:, 6], ALU.add))
                step(e.tensor_copy(sp[:, 0], sp[:, 7]))

            series, ser = log1p_step, [0]
            softplus()

            def chunk(c, first, more):
                for k in range(KD):
                    e.wait_ge(hh_ready, KD * c + k + 1)
                    e.tensor_tensor(h_lo[:, k], xT[:, k], h_hi[:, k].bitcast(F32), ALU.subtract).then_inc(hl_ready, 1)
                for j in range(JT):
                    m = JT * c + j
                    lo = SMP if first else 0
                    x_a, g_a, qk, v_t = 5 * j, 5 * j + 1, (5 * j + 2, 5 * j + 3), 5 * j + 4
                    ahead(c, x_a, more)
                    e.wait_ge(tap0_done, m + 1)
                    for i in range(1, CONV_A):
                        if first:
                            v = xc[j % 2][:, 0:SMP].rearrange("p (n s) -> p n s", s=SS)
                            if i > 1:
                                e.wait_ge(smp_tap, 3 * m + i - 1)
                            e.scalar_tensor_tensor(out=v, in0=sx[:, j, :, i:i + SS], scalar=lru_v[:, 4 + i, j:j + 1], in1=v,
                                                   op0=ALU.mult, op1=ALU.add).then_inc(smp_tap, 1)
                        if i > 1:
                            e.wait_ge(taps, 3 * m + i - 1)
                        e.scalar_tensor_tensor(out=xc[j % 2][:, lo:], in0=xe[j][:, lo + i:C + i], scalar=lru_v[:, 4 + i, j:j + 1],
                                               in1=xc[j % 2][:, lo:], op0=ALU.mult, op1=ALU.add).then_inc(taps, 1)
                    if j == 3 and more:
                        norm_scale(c + 1, (0, 1))
                    ahead(c, g_a, more)
                    e.wait_ge(xch_ready, m + 1)
                    e.tensor_tensor(xc_lo[:], xc[j % 2][:], xc_hi[:].bitcast(F32), ALU.subtract).then_inc(xcl_ready, 1)
                    if j == 3 and more:
                        norm_scale(c + 1, (2, 3, 4))
                    for i, t in enumerate(qk):
                        ahead(c, t, more)
                        if i == 1:
                            e.wait_ge(t_ready, m + 1)
                            if not (first and j < 2):
                                e.wait_ge(ya_stored[j % 2], 32 * c + 16 * (j // 2))
                            e.tensor_scalar(d_[j % 2][:], r_[:], 1.0, None, ALU.add).then_inc(d1_ready, 1)
                            e.wait_ge(d1_ready, m + 1)
                            e.reciprocal(d_[j % 2][:], d_[j % 2][:]).then_inc(d_ready, 1)
                            e.wait_ge(d_ready, m + 1)
                            e.tensor_scalar(a_[:], d_[j % 2][:], 2.0, -1.0, ALU.mult, ALU.add).then_inc(lru_a, 1)
                        if not (first and j == 0):
                            e.wait_ge(roped, 2 * m + i - 1)
                        e.wait_ge(rope_loaded, 16 * c + 16)
                        e.wait_ge(evacuated[t % 4], 5 * c + t // 4 + 1)
                        q = 2 * j + i
                        e.tensor_tensor((qT if q < JT else kT)[:, q % JT, cols(c)], raw[i][:], rope[:, 0], ALU.mult)
                        e.stream_shuffle(sh[i][:], raw[i][:], SWAP).then_inc(shuffled, 1)
                        if i == 0 and j == 3 and more:
                            norm_scale(c + 1, (5, 6, 7))
                    ahead(c, v_t, more)
                    e.wait_ge(u_ready, m + 1)
                    e.wait_ge(lru_a, m + 1)
                    if first:
                        v = lambda x: x[:, 0:SMP].rearrange("p (n s) -> p n s", s=SS)
                        flat = lambda x: x[:].rearrange("p n s -> p (n s)")
                        e.tensor_copy(a5[:, :, 1:], v(a_)).then_inc(smp_step, 1)
                        e.tensor_copy(u5[:, :, 1:], v(gi)).then_inc(smp_step, 1)
                        e.tensor_copy(u5[:, :, 0], h0[:, j]).then_inc(smp_step, 1)
                        e.wait_ge(smp_step, 6 * j + 3)
                        e.tensor_tensor_scan(flat(h5), flat(a5), flat(u5), 0.0, ALU.mult, ALU.add).then_inc(smp_step, 1)
                        e.wait_ge(smp_step, 6 * j + 4)
                        e.tensor_copy(v(r_), h5[:, :, 1:]).then_inc(smp_step, 1)
                        e.tensor_copy(hs_o[:, j], h5[:, :, SS]).then_inc(smp_step, 1)
                        e.wait_ge(smp_step, 6 * j + 6)
                        e.tensor_tensor_scan(r_[:, SMP:], a_[:, SMP:], gi[:, SMP:], 0.0, ALU.mult, ALU.add).then_inc(h_ready, 1)
                    else:
                        e.wait_ge(h_carried, m - JT + 1)
                        e.tensor_tensor_scan(r_[:], a_[:], gi[:], h_car[:, j:j + 1], ALU.mult, ALU.add).then_inc(h_ready, 1)
                    e.wait_ge(h_ready, m + 1)
                    e.tensor_copy(h_car[:, j:j + 1], r_[:, C - 1:C]).then_inc(h_carried, 1)
                    if j == 2 and more:
                        e.wait_ge(rms_ready, c + 2)
                        e.reciprocal(rstd[:], rstd[:]).then_inc(rstd_ready, 1)
                        e.wait_ge(rstd_ready, c + 2)

            chunks(e, chunk)

            e.wait_ge(band_ready, 1)

            def mask_max(b, t):
                u = 4 * b.idx + t
                e.wait_ge(qk_done, u + 1)
                if not (isinstance(u, int) and u < 4):
                    e.wait_ge(tr_done, u - 3)
                if t == 0 and b.order == 2 and not (isinstance(b.idx, int) and b.idx < 36):
                    e.wait_ge(cm_step, 11 * (b.idx - 35))
                k0 = 0 if b.prev else P
                e.sem_inc(dve_passed, 1)
                for hd in range(2):
                    ins = e.tensor_tensor_reduce(pm[t][:, hd, k0:], bank[t][:, 2 * P * hd + k0:2 * P * (hd + 1)], band[:, k0:],
                                                 1.0, NEG, ALU.add, ALU.max, st[:, b.n, 0, 2 * t + hd:2 * t + hd + 1])
                ins.then_inc(maxed, 1)
                e.wait_ge(maxed, u + 1)
                e.tensor_scalar(nm[:, t], st[:, b.n, 0, 2 * t:2 * t + 2], -SCALE, None, ALU.mult).then_inc(masked, 1)

            def wide(w):
                return w.rearrange("p (h o) -> p h o", o=1).broadcast_to([P, HEADS, HD])

            def heads(x):
                return x.rearrange("p (h d) -> p h d", d=HD)

            def combine_max(y, n):
                e.wait_ge(oc_loaded[n % 2], 8 * (y - n % 2) + 16)
                if not (isinstance(y, int) and y == 0):
                    e.wait_ge(cm_step, 11 * y)
                e.tensor_tensor(cm[:], oc[n % 2][:, 0, D_ATT:D_ATT + HEADS], oc[n % 2][:, 1, D_ATT:D_ATT + HEADS], ALU.max).then_inc(cm_max, 1)
                e.wait_ge(cm_max, 2 * y + 1)
                e.tensor_tensor(cm[:], cm[:], st[:, n, 0], ALU.max).then_inc(cm_max, 1)

            def combine_rec(y):
                e.wait_ge(cm_step, 11 * y + 8)
                e.reciprocal(cd[:], cd[:]).then_inc(cm_rec, 1)

            def combine_scale(y, par):
                e.wait_ge(cm_step, 11 * y + 9)
                e.tensor_tensor(heads(oc[par][:, 1, 0:D_ATT]), heads(oc[par][:, 1, 0:D_ATT]), wide(ce[:, 1]), ALU.mult).then_inc(cm_dve, 1)
                e.tensor_tensor(heads(ob[par][:, 0:D_ATT]), heads(ob[par][:, 0:D_ATT]), wide(ce[:, 2]), ALU.mult).then_inc(cm_dve, 1)

            def combine_add(y, par):
                e.wait_ge(cm_step, 11 * y + 11)
                e.tensor_tensor(ob[par][:, 0:D_ATT], ob[par][:, 0:D_ATT], oc[par][:, 1, 0:D_ATT], ALU.add).then_inc(cm_dve, 1)

            def sample_step(g, t):
                def step(ins, n):
                    ins.then_inc(sm_step, 1)
                    e.wait_ge(sm_step, 8 * g + n)

                if t == 1:
                    e.wait_ge(st_turned, g + 1)
                    e.wait_ge(smp_loaded, 48)
                    if g:
                        e.wait_ge(p_turned, g)
                    e.tensor_tensor_reduce(smp_p[:, 0:3 * P], bank[7][:, 0:3 * P], past_mask[:], 1.0, NEG, ALU.add, ALU.max,
                                           smp_m[:, 0:1]).then_inc(sm_step, 1)
                    new = bank[7][:, 3 * P:3 * P + SMP].rearrange("p (o k) -> p o k", o=1).broadcast_to([P, 3, SMP])
                    step(e.tensor_tensor_reduce(smp_p[:, 3 * P:].rearrange("p (o k) -> p o k", o=3), new, new_mask[:, g], 1.0, NEG,
                                                ALU.add, ALU.max, smp_m[:, 1:2]), 2)
                    step(e.tensor_tensor(smp_m[:, 0:1], smp_m[:, 0:1], smp_m[:, 1:2], ALU.max), 3)
                    step(e.tensor_scalar(smp_m[:, 2:3], smp_m[:, 0:1], -SCALE, None, ALU.mult), 4)
                if t == 2:
                    e.wait_ge(sm_exp, g + 1)
                    step(e.reciprocal(smp_m[:, 3:4], smp_m[:, 3:4]), 5)
                    step(e.tensor_scalar(smp_p[:], smp_p[:], smp_m[:, 3:4], None, ALU.mult), 6)
                    new = [smp_p[:, 3 * P + SMP * i:3 * P + SMP * (i + 1)] for i in range(3)]
                    step(e.tensor_tensor(new[1], new[1], new[2], ALU.add), 7)
                    e.tensor_tensor(new[0], new[0], new[1], ALU.add).then_inc(sm_step, 1)

            def body(cur, nxt, unit):
                y = cur.idx - 32
                par = cur.n % 2
                again = cur.order == 2 and not (isinstance(y, int) and y < 1)
                for t in range(4):
                    b, i = ahead_by(cur, nxt, t, 3)
                    if b:
                        mask_max(b, i)
                    if unit == "values" and cur.idx % 16 == 8:
                        sample_step(cur.order, t)
                    if again and t == 0:
                        combine_max(y - 1, (cur.n - 1) % 4)
                    if again and t == 1:
                        combine_rec(y - 1)
                    if again and t == 2:
                        combine_scale(y - 1, 1 - par)
                    if again and t == 3:
                        combine_add(y - 1, 1 - par)
                e.wait_ge(pv_done, 4 * cur.idx + 4)
                if cur.order < 2 or isinstance(y, int) and y < 2:
                    e.wait_ge(os_stored[par], 16 * (2 * cur.turn + cur.n // 2))
                else:
                    e.wait_ge(y_turned, y - 1)
                if cur.order < 2:
                    e.tensor_copy(ob[par][:, D_ATT:].rearrange("p (s h) -> p s h", s=2), st[:, cur.n])
                e.tensor_copy(ob[par][:, 0:D_ATT], bank[6][:]).then_inc(o_out, 1)

            for t in range(3):
                mask_max(blk(0, 0, 0), t)
            attention(e, body)
            combine_max(15, 3)
            combine_rec(15)
            combine_scale(15, 1)
            combine_add(15, 1)

            def ahead_c(n, t):
                split_lo(n + t + AHEAD, (t + AHEAD) % RING)

            def part_lo(g, k, src):
                e.wait_ge(hbh_ready, KD * g + k + 1)
                e.tensor_tensor(hb_lo[:, k], src, hb_hi[:, k].bitcast(F32), ALU.subtract).then_inc(hbl_ready, 1)

            def rstd_of(q):
                e.wait_ge(frms_ready, q + 1)
                e.reciprocal(rstd[:], rstd[:]).then_inc(frstd_ready, 1)
                e.wait_ge(frstd_ready, q + 1)

            def heads_product(c):
                e.wait_ge(tile_done, tile_out(c))
                for k in range(KD):
                    part_lo(2 * c, k, x1[:, k])
                for d in range(W_OUT):
                    ahead_c(tile_out(c), d)
                    e.wait_ge(tile_done, tile_out(c) + d + 1)
                    e.wait_ge(xs_loaded[d % 2], 64 * c + 16 * (d // 2) + 16)
                    e.tensor_tensor(x1[:, d], bank[d % 4][:, 0:C], xs[d % 2][:], ALU.add).then_inc(evacuated[d % 4], 1)

            def normed(c, k):
                if k >= 2:
                    e.wait_ge(hbl_ready, KD * (2 * c + 1) + k - 1)
                e.scalar_tensor_tensor(out=uc[k % 2][:], in0=x1[:, k], scalar=gains[:, 1, k:k + 1], in1=rstd[:],
                                       op0=ALU.mult, op1=ALU.mult).then_inc(fhn_ready, 1)

            def final(k):
                e.scalar_tensor_tensor(out=res[:, k], in0=res[:, k], scalar=gains[:, 2, k:k + 1], in1=rstd[:],
                                       op0=ALU.mult, op1=ALU.mult).then_inc(final_ready, 1)

            def ffn_chunk(c, first, more):
                n = tile_c(c, 0)
                for t in range(W_FFN):
                    f = t // 2
                    F = FT * c + f
                    u = f % 2
                    lo = SMP if first else 0
                    ahead_c(n, t)
                    if t % 2 == 0:
                        if f > 0:
                            e.wait_ge(ffh_ready, F)
                            e.tensor_tensor(ff_lo[:, f - 1], uc[1 - u][:], ff_hi[:, f - 1].bitcast(F32), ALU.subtract).then_inc(ffl_ready, 1)
                        e.wait_ge(ftap0, F + 1)
                        for i in range(1, CONV_F):
                            if first:
                                v = uc[u][:, 0:SMP].rearrange("p (n s) -> p n s", s=SS)
                                if i > 1:
                                    e.wait_ge(stap, 2 * F + 1)
                                e.scalar_tensor_tensor(out=v, in0=gs[u][:, :, i:i + SS], scalar=cf[:, 1 + i, f:f + 1], in1=v,
                                                       op0=ALU.mult, op1=ALU.add).then_inc(stap, 1)
                            if i > 1:
                                e.wait_ge(ftaps, 2 * F + 1)
                            e.scalar_tensor_tensor(out=uc[u][:, lo:], in0=gx[u][:, lo + i:C + i], scalar=cf[:, 1 + i, f:f + 1],
                                                   in1=uc[u][:, lo:], op0=ALU.mult, op1=ALU.add).then_inc(ftaps, 1)
                    else:
                        e.wait_ge(tile_done, n + t + 1)
                        e.wait_ge(gelu_done, F + 1)
                        e.tensor_tensor(uc[u][:], bank[t % 4][:, 0:C], uc[u][:], ALU.mult).then_inc(evacuated[t % 4], 1)
                    if t == 3 and not first:
                        rstd_of(2 * c)
                    if 4 <= t < 4 + KD and not first:
                        final(t - 4)
                e.wait_ge(ffh_ready, FT * c + FT)
                e.tensor_tensor(ff_lo[:, FT - 1], uc[1][:], ff_hi[:, FT - 1].bitcast(F32), ALU.subtract).then_inc(ffl_ready, 1)
                if more:
                    heads_product(c + 1)
                n = tile_c(c, W_FFN + (W_OUT if more else 0))
                for s in range(W_DOWN):
                    if more or s < W_DOWN - AHEAD:
                        ahead_c(n, s)
                    if more and s == 3:
                        rstd_of(norm_in(c + 1))
                    if more and 5 <= s < 5 + KD:
                        part_lo(2 * c + 3, s - 5, uc[(s - 5) % 2][:])
                    if more and 4 <= s < 4 + KD:
                        normed(c + 1, s - 4)
                    if s % 3 == 2:
                        d = s // 3
                        e.wait_ge(tile_done, n + s + 1)
                        if d == 0:
                            e.wait_ge(res_copied, KD * (c + 1))
                        e.tensor_tensor(res[:, d], bank[d % 4][:, 0:C], res[:, d], ALU.add).then_inc(evacuated[d % 4], 1)

            e.wait_ge(c_free, 1)
            heads_product(0)
            rstd_of(0)
            for k in range(KD):
                normed(0, k)
                if k > 0:
                    part_lo(1, k - 1, uc[(k - 1) % 2][:])
            part_lo(1, KD - 1, uc[1][:])
            chunks(e, ffn_chunk)
            rstd_of(norm_out(CHUNKS - 1, False))
            for k in range(KD):
                final(k)

        @block.gpsimd
        def _(e):
            def square_sum(c, ks):
                base = (2 * KD - 1) * c
                for k in ks:
                    if k == 0:
                        e.wait_ge(xt_loaded, 16 * c + 16)
                        if not (isinstance(c, int) and c == 0):
                            e.wait_ge(ms_ready, c)
                        e.tensor_tensor(ssq[:], xT[:, 0], xT[:, 0], ALU.mult).then_inc(sq_step, 1)
                    else:
                        e.tensor_tensor(sq[k % 2][:], xT[:, k], xT[:, k], ALU.mult).then_inc(sq_step, 1)
                        e.wait_ge(sq_step, base + 2 * k)
                        e.tensor_tensor(ssq[:], ssq[:], sq[k % 2][:], ALU.add).then_inc(sq_step, 1)

            def store_ya(c, j):
                e.dma_start(a["ya"][:, j, cols(c)], d_[j % 2][:]).then_inc(ya_stored[j % 2], 16)

            def store_k(c):
                e.dma_start(o["k"][:, :, cols(c)], kT[:, :, cols(c)]).then_inc(k_stored, 16)

            e.memset(ident[:], 0.0).then_inc(made, 1)
            e.memset(band[:], 0.0).then_inc(made, 1)
            e.wait_ge(made, 2)
            e.affine_select(out=ident[:], in_=ident[:], compare_op=ALU.not_equal, fill=1.0, base=0,
                            pattern=[[-1, P]], channel_multiplier=1).then_inc(ident_ready, 1)
            e.affine_select(out=band[:], in_=band[:], compare_op=ALU.is_ge, fill=NEG, base=0,
                            pattern=[[1, 2 * P]], channel_multiplier=-1).then_inc(made, 1)
            e.wait_ge(made, 3)
            e.affine_select(out=band[:], in_=band[:], compare_op=ALU.is_ge, fill=NEG, base=P,
                            pattern=[[-1, 2 * P]], channel_multiplier=1).then_inc(band_ready, 1)
            square_sum(0, range(KD))

            def chunk(c, first, more):
                for j in range(JT):
                    m = JT * c + j
                    if more and j < 2:
                        square_sum(c + 1, range(KD)[4 * j:4 * j + 4])
                    for i in range(2):
                        q = 2 * j + i
                        if i == 0 and not (first and j == 0):
                            e.wait_ge(ya_ready, m)
                        e.wait_ge(shuffled, 2 * m + i + 1)
                        e.tensor_tensor(sh[i][:], sh[i][:], rope[:, 1], ALU.mult).then_inc(sin_done, 1)
                        if i == 0 and j > 0:
                            store_ya(c, j - 1)
                        elif i == 0 and not first:
                            store_ya(c - 1, JT - 1)
                            store_k(c - 1)
                        if i == 1:
                            e.wait_ge(gi_ready, m + 1)
                            e.tensor_tensor(gi[:], gi[:], xc[j % 2][:], ALU.mult).then_inc(u1_ready, 1)
                        dst = (qT if q < JT else kT)[:, q % JT, cols(c)]
                        e.wait_ge(sin_done, 2 * m + i + 1)
                        e.tensor_tensor(dst, dst, sh[i][:], ALU.add).then_inc(roped, 1)
                    e.wait_ge(s_ready, m + 1)
                    e.wait_ge(lru_a, m + 1)
                    e.tensor_tensor(d_[j % 2][:], d_[j % 2][:], r_[:], ALU.mult).then_inc(sd_ready, 1)
                    e.wait_ge(sd_ready, m + 1)
                    e.wait_ge(u1_ready, m + 1)
                    e.tensor_tensor(gi[:], gi[:], d_[j % 2][:], ALU.mult).then_inc(u_ready, 1)
                    e.wait_ge(u_ready, m + 1)
                    e.wait_ge(h_ready, m + 1)
                    e.wait_ge(evacuated[(5 * j + 1) % 4], 5 * c + (5 * j + 1) // 4 + 1)
                    e.tensor_tensor(d_[j % 2][:], r_[:], gl[j % 2][:], ALU.mult).then_inc(ya_ready, 1)
                if first:
                    e.wait_ge(smp_tap, 3 * JT)
                    e.tensor_copy(sx_o[:], sx[:, :, :, SS:]).then_inc(smp_copied, 2)

            chunks(e, chunk)
            e.wait_ge(ya_ready, JT * CHUNKS)
            store_ya(CHUNKS - 1, JT - 1)
            e.wait_ge(roped, 8 * CHUNKS)
            store_k(CHUNKS - 1)
            e.wait_ge(taps, 3 * JT * CHUNKS)
            for j in range(JT):
                ins = e.tensor_copy(xe_o[:, j], xe[j][:, C:C + HA])
            ins.then_inc(smp_copied, 1)

            e.wait_ge(k_stored, 16 * CHUNKS)
            e.wait_ge(ya_stored[0], 16 * 2 * CHUNKS)
            e.wait_ge(ya_stored[1], 16 * 2 * CHUNKS)
            e.wait_ge(v_stored, 16 * JT * CHUNKS)
            e.wait_ge(smp_copied, 3)
            e.wait_ge(tile_done, N_A)
            e.memset(qp[0][:], 0.0).then_inc(qp_zeroed, 1)
            e.memset(qp[1][:], 0.0).then_inc(qp_zeroed, 1)
            e.memset(smp_q[:], 0.0).then_inc(qp_zeroed, 1)
            e.wait_ge(qp_zeroed, 3)
            e.sem_inc(a_done, 1)

            def copy_q(b):
                for hd in range(2):
                    rows = slice(HD * hd, HD * hd + HD)
                    ins = e.tensor_copy(qp[b.n % 2][rows, :, hd, :], qT[rows, :, bass.ds(b.first, P, b.dil)])
                ins.then_inc(q_copied, 1)

            def combine(y, n):
                par = n % 2
                base = 11 * y
                m = [oc[par][:, 0, D_ATT:D_ATT + HEADS], oc[par][:, 1, D_ATT:D_ATT + HEADS], st[:, n, 0]]
                l = [oc[par][:, 0, D_ATT + HEADS:], oc[par][:, 1, D_ATT + HEADS:], st[:, n, 1]]
                e.wait_ge(q_copied, 48 if isinstance(y, int) and y >= 14 else y + 35)
                e.wait_ge(o_out, y + 33)
                e.wait_ge(oc_loaded[par], 8 * (y - par) + 16)
                e.wait_ge(cm_max, 2 * y + 2)
                if not (isinstance(y, int) and y == 0):
                    e.wait_ge(cm_dve, 3 * y)
                for p in range(3):
                    e.tensor_tensor(ce[:, p], m[p], cm[:], ALU.subtract).then_inc(cm_step, 1)
                e.wait_ge(cm_exp, y + 1)
                for p in range(3):
                    e.tensor_tensor(cw[:, p], ce[:, p], l[p], ALU.mult).then_inc(cm_step, 1)
                e.wait_ge(cm_step, base + 6)
                e.tensor_tensor(cd[:], cw[:, 0], cw[:, 1], ALU.add).then_inc(cm_step, 1)
                e.wait_ge(cm_step, base + 7)
                e.tensor_tensor(cd[:], cd[:], cw[:, 2], ALU.add).then_inc(cm_step, 1)
                e.wait_ge(cm_rec, y + 1)
                e.tensor_tensor(ce[:], ce[:], cd[:].rearrange("p (o h) -> p o h", o=1).broadcast_to([P, 3, HEADS]), ALU.mult).then_inc(cm_step, 1)
                e.wait_ge(cm_step, base + 9)
                o2 = oc[par][:, 0, 0:D_ATT]
                e.tensor_tensor(o2.rearrange("p (h d) -> p h d", d=HD), o2.rearrange("p (h d) -> p h d", d=HD),
                                ce[:, 0].rearrange("p (h o) -> p h o", o=1).broadcast_to([P, HEADS, HD]), ALU.mult).then_inc(cm_step, 1)
                e.wait_ge(cm_step, base + 10)
                e.wait_ge(cm_dve, 3 * y + 2)
                e.tensor_tensor(ob[par][:, 0:D_ATT], ob[par][:, 0:D_ATT], o2, ALU.add).then_inc(cm_step, 1)

            def body(cur, nxt, unit):
                y = cur.idx - 32
                if nxt:
                    e.wait_ge(qk_done, 4 * cur.idx)
                    if cur.order == 2 and not (isinstance(y, int) and y < 2):
                        e.wait_ge(cm_step, 11 * (y - 1))
                    copy_q(nxt)
                if cur.order == 2 and not (isinstance(y, int) and y < 1):
                    combine(y - 1, (cur.n - 1) % 4)

            for hd in range(2):
                rows = slice(HD * hd, HD * hd + HD)
                ins = e.tensor_copy(smp_q[rows, :, :, hd], qT[rows, :, 0:SMP])
            ins.then_inc(smp_q_ready, 1)
            copy_q(blk(0, 0, 0))
            attention(e, body)
            combine(15, 3)

            e.wait_ge(y_turned, 16)
            e.wait_ge(yt_ready, 16)
            e.wait_ge(cm_dve, 48)
            e.wait_ge(smp_stored, 32)
            e.wait_ge(cm_step, 11 * 16)
            for i in range(2):
                e.wait_ge(yt_stored[i], 16 * 8)
            e.sem_inc(c_free, 1)
            for i in range(2):
                e.memset(gx[i][:, 0:HF + SMP], 0.0).then_inc(zeroed, 1)

            def square_sum_c(q, k, x, ev, count):
                base = (2 * KD - 1) * q
                e.wait_ge(evacuated[ev], count)
                if k == 0:
                    if not (isinstance(q, int) and q == 0):
                        e.wait_ge(fms_ready, q)
                    e.tensor_tensor(ssf[:], x, x, ALU.mult).then_inc(fsq_step, 1)
                else:
                    e.tensor_tensor(sqf[k % 2][:], x, x, ALU.mult).then_inc(fsq_step, 1)
                    e.wait_ge(fsq_step, base + 2 * k)
                    e.tensor_tensor(ssf[:], ssf[:], sqf[k % 2][:], ALU.add).then_inc(fsq_step, 1)

            def passed():
                e.sem_inc(pool_passed, 1)

            def halo(c, first, f):
                F = FT * c + f
                if not (first and f < 2):
                    e.wait_ge(ftaps, 2 * F - 2)
                if first:
                    if f == 0:
                        e.wait_ge(cf_loaded, 32)
                        e.wait_ge(zeroed, 2)
                    else:
                        e.wait_ge(halo_ready, F)
                    passed()
                    e.tensor_copy(gs[f % 2][:, :, 0:HF], sf[:, f]).then_inc(halo_ready, 1)
                else:
                    e.wait_ge(carried, F - FT + 1)
                    passed()
                    e.tensor_copy(gx[f % 2][:, 0:HF], carry[:, f]).then_inc(halo_ready, 1)

            def ffn_chunk(c, first, more):
                halo(c, first, 0)
                for f in range(FT):
                    F = FT * c + f
                    if f + 1 < FT:
                        halo(c, first, f + 1)
                    e.wait_ge(halo_ready, F + 1)
                    e.wait_ge(evacuated[2 * f % 4], ev_ffn(c) + f // 2 + 1)
                    passed()
                    if first:
                        e.tensor_copy(sf[:, f], gs[f % 2][:, :, SS:])
                    e.tensor_copy(carry[:, f], gx[f % 2][:, C:]).then_inc(carried, 1)
                    if 8 <= f < 8 + KD:
                        k = f - 8
                        if not first and k == 0:
                            e.wait_ge(final_stored, 16 * c)
                            passed()
                        e.tensor_copy(res[:, k], x1[:, k]).then_inc(res_copied, 1)
                if more:
                    for d in range(W_OUT):
                        square_sum_c(norm_in(c + 1), d, x1[:, d], d % 4, ev_out(c + 1) + d // 4 + 1)
                for d in range(KD):
                    square_sum_c(norm_out(c, more), d, res[:, d], d % 4, ev_down(c, more) + d // 4 + 1)

            for d in range(W_OUT):
                square_sum_c(0, d, x1[:, d], d % 4, ev_out(0) + d // 4 + 1)
            chunks(e, ffn_chunk)

        @block.tensor
        def _(e):
            def product(out, s, k, hi, lo, start, stop):
                e.matmul(out, w_hi[s][:, k], hi, start=start, stop=False)
                e.matmul(out, w_hi[s][:, k], lo, start=False, stop=False)
                return e.matmul(out, w_lo[s][:, k], hi, start=False, stop=stop)

            def mean_square(c):
                e.wait_ge(sq_step, (2 * KD - 1) * (c + 1))
                if not (isinstance(c, int) and c == 0):
                    e.wait_ge(rms_ready, c)
                e.matmul(bank[4][:, 0:C], ones[:], ssq[:], start=True, stop=True).then_inc(ms_ready, 1)

            def turn_v(m, b, n):
                e.wait_ge(evacuated[b], n)
                if not (isinstance(m, int) and m == 0):
                    e.wait_ge(v_ready, m)
                for i in range(C // VR):
                    last = e.transpose(bank[7][0:VR, i * P:(i + 1) * P], v_cols[:, i * VR:(i + 1) * VR], ident[:])
                last.then_inc(v_turned, 1)

            e.wait_ge(par_ready, 1)
            e.wait_ge(ident_ready, 1)
            mean_square(0)

            def chunk(c, first, more):
                for t in range(W_IN):
                    n = c * W_IN + t
                    e.wait_ge(lo_ready, n + 1)
                    if not (first and t < 4):
                        e.wait_ge(evacuated[t % 4], 5 * c + t // 4)
                    for k in range(KD):
                        if t == 0:
                            e.wait_ge(hl_ready, KD * c + k + 1)
                        last = product(bank[t % 4][:, 0:C], t % RING, k, h_hi[:, k], h_lo[:, k], k == 0, k == KD - 1)
                    last.then_inc(tile_done, 1)
                    if t % 5 == 2:
                        j = t // 5
                        m = JT * c + j
                        e.wait_ge(xcl_ready, m + 1)
                        if first and j == 0:
                            e.wait_ge(gw_ready, 1)
                        if not (first and j == 0):
                            e.wait_ge(r_ready, m)
                            e.wait_ge(gi_ready, m)
                        for g in range(2):
                            out = bank[5 + g][:, 0:C]
                            e.matmul(out, gw_hi[:, g, j], xc_hi[:], start=True, stop=False)
                            e.matmul(out, gw_hi[:, g, j], xc_lo[:], start=False, stop=False)
                            last = e.matmul(out, gw_lo[:, g, j], xc_hi[:], start=False, stop=True)
                        last.then_inc(gates_done, 1)
                    if t == 12 and more:
                        mean_square(c + 1)
                    if t % 5 == 0 and not (first and t == 0):
                        turn_v(JT * c + t // 5 - 1, *((t - 1) % 4, 5 * c + (t - 1) // 4 + 1))

            chunks(e, chunk)
            turn_v(JT * CHUNKS - 1, 3, 5 * CHUNKS)

            def scores(b, t):
                u = 4 * b.idx + t
                if t == 0:
                    e.wait_ge(q_copied, b.idx + 1)
                if not (isinstance(u, int) and u < 4):
                    e.wait_ge(masked, u - 3)
                n = 2 * P if b.prev else P
                keys = bass.ds(b.first - P * b.dil if b.prev else b.first, n, b.dil)
                for hd in range(2):
                    last = e.matmul(bank[t][:, 2 * P * (hd + 1) - n:2 * P * (hd + 1)], qp[b.n % 2][:, t, hd], kT[:, t, keys],
                                    start=True, stop=True)
                last.then_inc(qk_done, 1)

            def turn(b, t):
                u = 4 * b.idx + t
                e.wait_ge(exp_done, u + 1)
                if not (isinstance(u, int) and u < 2):
                    e.wait_ge(pt_ready, u - 1)
                for hd in range(2):
                    for kb in range(0 if b.prev else 1, 2):
                        i = 2 * hd + kb
                        last = e.transpose(bank[4 + t % 2][:, i * P:(i + 1) * P], pm[t][:, hd, kb * P:(kb + 1) * P], ident[:])
                last.then_inc(tr_done, 1)

            def values(b, t):
                u = 4 * b.idx + t
                e.wait_ge(pt_ready, u + 1)
                if t == 0:
                    e.wait_ge(vb_loaded[b.n], 16 * b.turn + 16)
                    e.wait_ge(o_out, b.idx)
                for hd in range(2):
                    h = slice((2 * t + hd) * HD, (2 * t + hd + 1) * HD)
                    if b.prev:
                        e.matmul(bank[6][:, h], pt[t % 2][:, hd, 0], vb[:, (b.n - 1) % 4, h], start=True, stop=False)
                    last = e.matmul(bank[6][:, h], pt[t % 2][:, hd, 1], vb[:, b.n, h], start=not b.prev, stop=True)
                last.then_inc(pv_done, 1)

            def turn_y(y, par):
                e.wait_ge(cm_dve, 3 * y + 3)
                if not (isinstance(y, int) and y < 1):
                    e.wait_ge(yt_ready, y)
                else:
                    e.wait_ge(smp_y_ready, 2)
                for j in range(JT):
                    last = e.transpose(bank[7][:, j * P:(j + 1) * P], ob[par][:, j * P:(j + 1) * P], ident[:])
                last.then_inc(y_turned, 1)

            def sample_keys(b):
                e.wait_ge(past_loaded[b.n], 16 * b.turn + 16)
                if b.n == 0:
                    e.wait_ge(smp_q_ready, 1)
                    if b.order:
                        e.wait_ge(smp_y_ready, b.order)
                    else:
                        e.wait_ge(v_ready, JT * CHUNKS)
                for i in range(2):
                    t = 2 * (b.n % 2) + i
                    seq = 2 * b.k + b.n // 2
                    for blk_ in range(PAST_KEYS):
                        pat, tok, cnt = (0, 0, SS) if blk_ == 0 else ((blk_ + 3) // 4, (blk_ - 1) % 4, 1)
                        out = bank[7][:, bass.ds(P * pat + 32 * seq + 8 * tok, 8 * cnt)].rearrange("p (s h) -> p s h", h=HEADS)[:, :, 2 * t:2 * t + 2]
                        last = e.matmul(out, past[b.n][:, i, blk_ * P:(blk_ + 1) * P],
                                        smp_q[:, t, bass.ds(16 * b.order + 4 * seq + tok, cnt), :], start=True, stop=True)
                last.then_inc(past_used, 1)

            def group(x):
                return x.rearrange("p (k h) -> p k h", h=HEADS)

            def sample_step(g, i):
                if i == 0:
                    for t in range(JT):
                        last = e.matmul(group(bank[7][0:SMP, 3 * P:])[:, :, 2 * t:2 * t + 2], kT[:, t, 0:SMP],
                                        smp_q[:, t, 16 * g:16 * g + 16, :], start=True, stop=True)
                    last.then_inc(new_scored, 1)
                if i == 1:
                    e.wait_ge(st_copied, g + 1)
                    for p in range(3):
                        e.transpose(bank[7][:, p * P:(p + 1) * P], turned_s[:, p * P:(p + 1) * P], ident[:])
                    e.transpose(bank[7][:, 3 * P:3 * P + SMP], turned_s[0:SMP, 3 * P:], ident[0:SMP, 0:SMP]).then_inc(st_turned, 1)
                if i == 3:
                    e.wait_ge(sm_step, 8 * g + 8)
                    for p in range(3):
                        e.transpose(bank[7][:, p * P:(p + 1) * P], smp_p[:, p * P:(p + 1) * P], ident[:])
                    e.transpose(bank[7][0:SMP, 3 * P:], smp_p[:, 3 * P:3 * P + SMP], ident[:]).then_inc(p_turned, 1)

            def sample_values(b):
                if b.idx % 16 == 8:
                    e.wait_ge(pt_copied, b.order + 1)
                e.wait_ge(past_loaded[b.n], 16 * b.turn + 16)
                for i in range(2):
                    t = 2 * (b.n % 2) + i
                    seq = 2 * (b.k - 2) + b.n // 2

                    def add(lhs, keys, pat, tok, cnt, start, stop):
                        at = 32 * t + 8 * seq + 2 * tok
                        row = P * pat + 32 * seq + 8 * tok
                        return e.matmul(bank[7][:, at:at + 2 * cnt].rearrange("p (k d) -> p k d", d=2), lhs,
                                        group(turned_s[0:keys, row:row + 8 * cnt])[:, :, 2 * t:2 * t + 2], start=start, stop=stop)

                    add(v_new[:, t * P:(t + 1) * P], SMP, 3, 0, SS, True, False)
                    for kb in range(1, PAST_KEYS):
                        add(past[b.n][:, i, kb * P:(kb + 1) * P], P, (kb + 3) // 4, (kb - 1) % 4, 1, False, False)
                    last = add(past[b.n][:, i, 0:P], P, 0, 0, SS, False, True)
                last.then_inc(past_used, 1)

            def body(cur, nxt, unit):
                y = cur.idx - 32
                for t in range(4):
                    if unit == "values" and cur.idx % 16 == 8:
                        sample_step(cur.order, t)
                    b, i = ahead_by(cur, nxt, t, 3)
                    if b:
                        scores(b, i)
                    b, i = ahead_by(cur, nxt, t, 1)
                    if b:
                        turn(b, i)
                    values(cur, t)
                    if cur.order == 2 and not (isinstance(y, int) and y < 2) and t == 0:
                        turn_y(y - 2, cur.n % 2)
                if unit == "keys":
                    sample_keys(cur)
                if unit == "values":
                    sample_values(cur)

            e.wait_ge(a_done, 1)
            for i in range(4):
                e.wait_ge(evacuated[i], 5 * CHUNKS)
            e.wait_ge(rms_ready, CHUNKS)
            e.wait_ge(gi_ready, JT * CHUNKS)
            for t in range(3):
                scores(blk(0, 0, 0), t)
            turn(blk(0, 0, 0), 0)
            attention(e, body)
            turn_y(14, 0)
            turn_y(15, 1)

            def mean_square_c(q):
                e.wait_ge(fsq_step, (2 * KD - 1) * (q + 1))
                if not (isinstance(q, int) and q == 0):
                    e.wait_ge(frms_ready, q)
                e.matmul(bank[4][:, 0:C], ones[:], ssf[:], start=True, stop=True).then_inc(fms_ready, 1)

            def dense(n, t, ev, g):
                e.wait_ge(lo_ready, n + t + 1)
                e.wait_ge(evacuated[t % 4], ev + t // 4)
                for k in range(KD):
                    if t == 0:
                        e.wait_ge(hbl_ready, KD * g + k + 1)
                    last = product(bank[t % 4][:, 0:C], t % RING, k, hb_hi[:, k], hb_lo[:, k], k == 0, k == KD - 1)
                last.then_inc(tile_done, 1)

            def ffn_chunk(c, first, more):
                for t in range(W_FFN):
                    dense(tile_c(c, 0), t, ev_ffn(c), 2 * c + 1)
                    if t == 1 and not first:
                        mean_square_c(2 * c)
                if more:
                    for d in range(W_OUT):
                        dense(tile_out(c + 1), d, ev_out(c + 1), 2 * c + 2)
                n = tile_c(c, W_FFN + (W_OUT if more else 0))
                for s in range(W_DOWN):
                    d, g = s // 3, s % 3
                    e.wait_ge(lo_ready, n + s + 1)
                    if d == 0:
                        e.wait_ge(ffl_ready, FT * c + KD * (g + 1))
                    if g == 0:
                        e.wait_ge(evacuated[d % 4], ev_down(c, more) + d // 4)
                    for k in range(KD):
                        last = product(bank[d % 4][:, 0:C], s % RING, k, ff_hi[:, KD * g + k], ff_lo[:, KD * g + k],
                                       g == 0 and k == 0, g == 2 and k == KD - 1)
                    last.then_inc(tile_done, 1)
                    if more and s == 1:
                        mean_square_c(norm_in(c + 1))

            e.wait_ge(c_free, 1)
            for d in range(W_OUT):
                dense(tile_out(0), d, ev_out(0), 0)
            mean_square_c(0)
            chunks(e, ffn_chunk)
            mean_square_c(norm_out(CHUNKS - 1, False))


Block = namedtuple("Block", "order idx turn k n first dil prev")
SWAP = [i + 8 if i < 8 else i - 8 if i < 16 else i for i in range(32)]


def column_tiles(w):
    k, n = w.shape
    return w.reshape(k // P, P, n // P, P).transpose(2, 1, 0, 3)


def by_channel(x):
    x = np.moveaxis(x, -1, 0)
    return x.reshape((x.shape[0] // P, P) + x.shape[1:]).swapaxes(0, 1)


def rotary_tables():
    half = ROT // 2
    inv = np.float32(500000.0) ** (np.float32(-2.0) * np.arange(half, dtype=np.float32) / np.float32(ROT))
    pos = np.concatenate([np.tile(PAST + np.arange(SS), NS), np.arange(SEQ)]).astype(np.float32)
    ang = inv.astype(np.float32)[:, None] * pos[None]
    out = np.zeros((P, 2, TOK), np.float32)
    out[:, 0] = 1.0
    for h in range(P // HD):
        for i in range(2):
            rows = slice(h * HD + i * half, h * HD + (i + 1) * half)
            out[rows, 0] = np.cos(ang)
            out[rows, 1] = np.sin(ang) * (1 if i else -1)
    return out


def past_blocks(x):
    n, w, ch = x.shape
    return np.concatenate([
        x[:, None, w - P:],
        x[:, w - 4 * P:].reshape(n, P, 4, ch).swapaxes(1, 2),
        x.reshape(n, P, 16, ch)[:, :, :SS].swapaxes(1, 2)], 1)


def past_units(k, v):
    k, v = past_blocks(k), past_blocks(v)
    k = k.reshape(2, 4, PAST_KEYS, P, 2, 2, P).transpose(0, 1, 4, 6, 5, 2, 3)
    v = v.reshape(2, 4, PAST_KEYS, P, 2, 2, P).transpose(0, 1, 4, 3, 5, 2, 6)
    return np.concatenate([x.reshape(2, 8, P, 2, PAST_KEYS * P) for x in (k, v)], 1).reshape(32, P, 2, PAST_KEYS * P)


def sample_masks():
    row = np.arange(P)
    seq, tok = row // 32, row // HEADS % SS
    past = np.zeros((P, 3 * P), np.float32)
    past[:, :P] = np.where(np.arange(P)[None] >= tok[:, None], 0.0, NEG)
    new = np.full((P, 2, 3, SMP), NEG, np.float32)
    key = np.arange(SMP)
    for g in range(2):
        mine = (key // SS)[None] == 4 * g + seq[:, None]
        new[:, g, 0][mine & ((key % SS)[None] <= tok[:, None])] = 0.0
        for p in (1, 2):
            new[:, g, p][mine & ((key % SS)[None] == tok[:, None])] = 0.0
    return past, new


def by_token(x):
    x = x.swapaxes(0, 1)
    return np.moveaxis(x.reshape((-1,) + x.shape[2:]), 0, -1)


def kernel(**inputs):
    import concourse.bacc as bacc
    from concourse.bass_utils import run_bass_kernel_spmd

    x = {k: np.asarray(v) for k, v in inputs.items()}
    tiles = column_tiles(x["w_in"][0])
    order = [y for j in range(JT) for y in (j, JT + j, 2 * JT + 2 * j, 2 * JT + 2 * j + 1, 4 * JT + j)]
    gate, up = column_tiles(x["w_ffn_gate"][0]), column_tiles(x["w_ffn_up"][0])
    down = x["w_ffn_down"][0].reshape(3, D, D)
    down = np.stack([column_tiles(down[g]) for g in range(3)], 1).reshape(W_DOWN, P, KD, P)
    arrays = {
        "x": by_channel(np.concatenate([x["x_sample"].reshape(SMP, D), x["x_prompt"][0]])),
        "w": np.concatenate([tiles[order], column_tiles(x["w_out"][0]), np.stack([gate, up], 1).reshape(W_FFN, P, KD, P), down]),
        "gains": by_channel(np.stack([x["g_mix"][0], x["g_ffn"][0], x["g_final"]])).swapaxes(1, 2),
        "lru_v": by_channel(np.concatenate([x["lru_b_r"], x["lru_b_i"], x["lru_lambda"], x["conv_a_b"], x["conv_a_w"][0]])).swapaxes(1, 2),
        "state_a": by_channel(x["state_conv_a"][0]),
        "h0": by_channel(x["state_lru_h"][0]),
        "gates_w": np.stack([x["lru_w_r"][0], x["lru_w_i"][0]]).reshape(2, JT, 2, HD, HD).transpose(0, 2, 3, 1, 4),
        "rope": rotary_tables(),
        "conv_f": by_channel(np.concatenate([x["conv_f_b"], x["conv_f_w"][0]])).swapaxes(1, 2),
        "state_f": by_channel(x["state_conv_ffn"][0]),
    }
    arrays["past"] = past_units(x["cache_win_k"][0].reshape(NS, -1, D_ATT), x["cache_win_v"][0].reshape(NS, -1, D_ATT))
    arrays["past_mask"], arrays["new_mask"] = sample_masks()
    outs = {
        "k": (P, JT, TOK), "v": (TOK, D_ATT), "y": (P, KD, TOK), "s_conv_a": (P, JT, NS, HA), "s_lru_h": (P, JT, NS),
        "p_conv_a": (P, JT, HA), "p_lru_h": (P, JT), "s_conv_f": (P, FT, NS, HF), "p_conv_f": (P, FT, HF),
    }
    nc = bacc.Bacc("TRN2", target_bir_lowering=False, num_devices=1)
    arrays = {k: np.ascontiguousarray(v) for k, v in arrays.items()}
    a = {k: nc.dram_tensor("in_" + k, v.shape, F32, kind="ExternalInput").ap() for k, v in arrays.items()}
    o = {k: nc.dram_tensor("out_" + k, s, F32, kind="ExternalOutput").ap() for k, s in outs.items()}
    a["os"] = nc.dram_tensor("attention_rows", (2, SEQ, OS), F32, kind="Internal").ap()
    a["ya"] = nc.dram_tensor("mixed_lru", (P, JT, TOK), F32, kind="Internal").ap()
    a["yb"] = nc.dram_tensor("mixed_attention", (P, JT, TOK), F32, kind="Internal").ap()
    build(nc, a, o)
    r = run_bass_kernel_spmd(nc, [{"in_" + k: v for k, v in arrays.items()}], core_ids=[0]).results[0]
    r = {k: r["out_" + k] for k in outs}
    y, k = by_token(r["y"]), by_token(r["k"])
    return (
        y[SMP:].reshape(1, SEQ, D), y[:SMP].reshape(NS, SS, D),
        by_token(r["p_conv_a"]).reshape(1, 1, HA, D_LRU), by_token(r["p_lru_h"]).reshape(1, 1, D_LRU),
        k[SMP:].reshape(1, 1, SEQ, HEADS, HD), r["v"][SMP:].reshape(1, 1, SEQ, HEADS, HD),
        by_token(r["p_conv_f"]).reshape(1, 1, HF, FF),
        by_token(r["s_conv_a"]).reshape(1, NS, HA, D_LRU), by_token(r["s_lru_h"]).reshape(1, NS, D_LRU),
        k[:SMP].reshape(1, NS, SS, HEADS, HD), r["v"][:SMP].reshape(1, NS, SS, HEADS, HD),
        by_token(r["s_conv_f"]).reshape(1, NS, HF, FF),
    )
```

```python
from collections import namedtuple
from contextlib import ExitStack

import numpy as np

import concourse.bass as bass
from concourse import mybir

F32 = mybir.dt.float32
F32R = mybir.dt.float32r
ALU = mybir.AluOpType
ACT = mybir.ActivationFunctionType
AX = mybir.AxisListType

P = 128
D = 1024
KD = D // P
D_LRU = 512
JT = D_LRU // P
FF = 3 * D
FT = FF // P
CONV_A, CONV_F = 4, 3
HA, HF = CONV_A - 1, CONV_F - 1
SEQ, NS, SS = 2048, 8, 4
SMP = NS * SS
TOK = SMP + SEQ
CHUNKS = 5
C = TOK // CHUNKS
VR = C // 4
PAST = 4096
EPS = 1e-6
HD, ROT, HEADS = 64, 16, 8
D_ATT = HEADS * HD
OS = D_ATT + 2 * HEADS
SCALE = HD ** -0.5
NEG = -1e30
PAST_KEYS = 9
LRU_C = 8.0

W_IN, W_OUT, W_FFN, W_DOWN = 20, KD, 2 * FT, KD * 3
T_IN, T_OUT, T_FFN, T_DOWN = 0, W_IN, W_IN + W_OUT, W_IN + W_OUT + W_FFN
SOFTPLUS_STEPS = 2 + 5 + 2 * 8 + 6
AHEAD = 3
RING = 4
STAGE = 4
N_A = CHUNKS * W_IN
N_ALL = N_A + CHUNKS * (W_OUT + W_FFN + W_DOWN)


def build(nc, a, o):
    with ExitStack() as ctx:
        def sb(name, shape, dt=F32, on=ctx):
            return on.enter_context(nc.sbuf_tensor(name, shape, dt))

        def sem(name):
            return ctx.enter_context(nc.semaphore(name))

        stage = [sb(f"stage{i}", [P, KD, P]) for i in range(STAGE)]
        w_hi = [sb(f"w_hi{i}", [P, KD, P], F32R) for i in range(RING)]
        w_lo = [sb(f"w_lo{i}", [P, KD, P], F32R) for i in range(RING)]
        ones = sb("ones", [P, P])
        gains = sb("gains", [P, 3, KD])
        eps = sb("eps", [P, 1])
        ident = sb("ident", [P, P])
        rstd = sb("rstd", [P, C])
        in_ab = ExitStack()
        qT = sb("qT", [P, JT, TOK], on=in_ab)
        kT = sb("kT", [P, JT, TOK], on=in_ab)
        band = sb("band", [P, 2 * P], on=in_ab)
        in_a = ExitStack()
        xT = sb("xT", [P, KD, C], on=in_a)
        h_hi = sb("h_hi", [P, KD, C], F32R, on=in_a)
        h_lo = sb("h_lo", [P, KD, C], F32R, on=in_a)
        xe = [sb(f"xe{j}", [P, HA + C], on=in_a) for j in range(JT)]
        sx = sb("sx", [P, JT, NS, HA + SS], on=in_a)
        gl = [sb(f"gl{i}", [P, C], on=in_a) for i in range(2)]
        xc = [sb(f"xc{i}", [P, C], on=in_a) for i in range(2)]
        xc_hi = sb("xc_hi", [P, C], F32R, on=in_a)
        xc_lo = sb("xc_lo", [P, C], F32R, on=in_a)
        r_ = sb("r_", [P, C], on=in_a)
        gi = sb("gi", [P, C], on=in_a)
        d_ = [sb(f"d{i}", [P, C], on=in_a) for i in range(2)]
        a_ = sb("a_", [P, C], on=in_a)
        raw = [sb(f"raw{i}", [P, C], on=in_a) for i in range(2)]
        with ExitStack() as in_g:
            gw = sb("gw", [P, 2, JT, P], on=in_g)
        v_cols = sb("v_cols", [P, C], on=in_a)
        v_rows = sb("v_rows", [VR, C // VR * P], on=in_a)
        sh = [sb(f"sh{i}", [P, C], on=in_a) for i in range(2)]
        rope = sb("rope", [P, 2, C], on=in_a)
        sq = sb("sq", [P, C], on=in_a)
        ssq = sb("ssq", [P, C], on=in_a)
        gw_hi = sb("gw_hi", [P, 2, JT, P], F32R, on=in_a)
        gw_lo = sb("gw_lo", [P, 2, JT, P], F32R, on=in_a)
        lru_v = sb("lru_v", [P, 4 + CONV_A, JT], on=in_a)
        sp = sb("sp", [P, 8, JT], on=in_a)
        h_car = sb("h_car", [P, JT], on=in_a)
        h0 = sb("h0", [P, JT, NS], on=in_a)
        a5 = sb("a5", [P, NS, SS + 1], on=in_a)
        u5 = sb("u5", [P, NS, SS + 1], on=in_a)
        h5 = sb("h5", [P, NS, SS + 1], on=in_a)
        hs_o = sb("hs_o", [P, JT, NS], on=in_a)
        sx_o = sb("sx_o", [P, JT, NS, HA], on=in_a)
        xe_o = sb("xe_o", [P, JT, HA], on=in_a)
        squares0 = [sq, d_[0], ssq, r_, gi, a_, raw[0], raw[1]]
        in_a.close()
        in_p = ExitStack()
        qp = [sb(f"qp{i}", [P, JT, 2, P], on=in_p) for i in range(2)]
        with ExitStack() as in_q:
            out_rows = sb("out_rows", [SMP, D_ATT], on=in_q)
        q_rows = sb("q_rows", [SMP, D_ATT], on=in_p)
        nm = sb("nm", [P, 4, 2], on=in_p)
        st = sb("st", [P, 4, 2, HEADS], on=in_p)
        pm = [sb(f"pm{i}", [P, 2, 2 * P], on=in_p) for i in range(4)]
        pt = [sb(f"pt{i}", [P, 2, 2, P], on=in_p) for i in range(2)]
        vb = sb("vb", [P, 4, D_ATT], on=in_p)
        ob = [sb(f"ob{i}", [P, OS], on=in_p) for i in range(2)]
        oc = [sb(f"oc{i}", [P, 2, OS], on=in_p) for i in range(2)]
        cm = sb("cm", [P, HEADS], on=in_p)
        ce = sb("ce", [P, 3, HEADS], on=in_p)
        cw = sb("cw", [P, 3, HEADS], on=in_p)
        cd = sb("cd", [P, HEADS], on=in_p)
        yt = [sb(f"yt{i}", [P, JT, P], on=in_p) for i in range(2)]
        past = [sb(f"past{i}", [P, 2 * PAST_KEYS * P], on=in_p) for i in range(2)]
        qb = [sb(f"qb{i}", [P, SS, D_ATT // 2], on=in_p) for i in range(2)]
        with ExitStack() as in_y:
            smp_y = sb("smp_y", [P, JT, SMP], on=in_y)
        prod = sb("prod", [P, SS, D_ATT // 2], on=in_p)
        smp_q = sb("smp_q", [P, JT, SMP, 2], on=in_p)
        v_new = sb("v_new", [SMP, D_ATT], on=in_p)
        past_mask = sb("past_mask", [P, 3 * P], on=in_p)
        new_mask = sb("new_mask", [P, 2, 3, SMP], on=in_p)
        turned_s = sb("turned_s", [P, 4, SMP * HEADS], on=in_p)
        spread = [sb(f"spread{i}", [P, 32 + 2 * SS * 40 + 32], on=in_p) for i in range(2)]
        smp_p = sb("smp_p", [P, 3 * P + 3 * SMP], on=in_p)
        smp_m = sb("smp_m", [P, 4], on=in_p)
        in_p.close()
        in_ab.close()
        in_c = ExitStack()
        x1 = sb("x1", [P, KD, C], on=in_c)
        hb_hi = sb("hb_hi", [P, KD, C], F32R, on=in_c)
        hb_lo = sb("hb_lo", [P, KD, C], F32R, on=in_c)
        xs = [sb(f"xs{i}", [P, C], on=in_c) for i in range(2)]
        uc = [sb(f"uc{i}", [P, C], on=in_c) for i in range(2)]
        sqf = [sb(f"sqf{i}", [P, C], on=in_c) for i in range(2)]
        ssf = sb("ssf", [P, C], on=in_c)
        gx = [sb(f"gx{i}", [P, HF + C], on=in_c) for i in range(2)]
        gs = [sb(f"gs{i}", [P, NS, HF + SS], on=in_c) for i in range(2)]
        cf = sb("cf", [P, 1 + CONV_F, FT], on=in_c)
        sf = sb("sf", [P, FT, NS, HF], on=in_c)
        carry = sb("carry", [P, FT, HF], on=in_c)
        res = sb("res", [P, KD, C], on=in_c)
        ff_hi = sb("ff_hi", [P, FT, C], F32R, on=in_c)
        ff_lo = sb("ff_lo", [P, FT, C], F32R, on=in_c)
        in_c.close()

        bank = [ctx.enter_context(nc.psum_tensor(f"bank{i}", [P, 512], F32)) for i in range(8)]

        w_loaded = [sem(f"w_loaded{i}") for i in range(STAGE)]
        hi_ready, lo_ready = sem("hi_ready"), sem("lo_ready")
        tile_done = sem("tile_done")
        evacuated = [sem(f"evacuated{i}") for i in range(4)]
        gains_loaded, par_loaded, par_ready = sem("gains_loaded"), sem("par_loaded"), sem("par_ready")
        gw_zeroed, gw_loaded, gw_split, gw_ready = sem("gw_zeroed"), sem("gw_loaded"), sem("gw_split"), sem("gw_ready")
        sp_step = sem("sp_step")
        x0_loaded, sq0_ready = [sem(f"x0_loaded{i}") for i in range(KD)], sem("sq0_ready")
        xt_loaded, sq_step, ms_ready, rms_ready, rstd_ready = (sem(x) for x in ("xt_loaded", "sq_step", "ms_ready", "rms_ready", "rstd_ready"))
        hn_ready, hh_ready, hl_ready = sem("hn_ready"), sem("hh_ready"), sem("hl_ready")
        xa_carried, tap0_done, taps, smp_tap = sem("xa_carried"), sem("tap0_done"), sem("taps"), sem("smp_tap")
        xch_ready, xcl_ready, gates_done, r_ready, gi_ready, t_ready = (sem(x) for x in ("xch_ready", "xcl_ready", "gates_done", "r_ready", "gi_ready", "t_ready"))
        d1_ready, d_ready, s_ready, lru_a, u1_ready, sd_ready, u_ready, h_ready, h_carried, ya_ready = (sem(x) for x in (
            "d1_ready", "d_ready", "s_ready", "lru_a", "u1_ready", "sd_ready", "u_ready", "h_ready", "h_carried", "ya_ready"))
        ya_stored = [sem(f"ya_stored{i}") for i in range(2)]
        smp_step, smp_copied = sem("smp_step"), sem("smp_copied")
        rope_loaded, shuffled, sin_done, roped = (sem(x) for x in ("rope_loaded", "shuffled", "sin_done", "roped"))
        v_stored, v_turned, v_ready = sem("v_stored"), sem("v_turned"), sem("v_ready")
        made, ident_ready, band_ready = sem("made"), sem("ident_ready"), sem("band_ready")
        (a_done, qp_zeroed, q_copied, qk_done, maxed, masked, exp_done, tr_done, pt_ready, pv_done, o_out) = (sem(x) for x in (
            "a_done", "qp_zeroed", "q_copied", "qk_done", "maxed", "masked", "exp_done", "tr_done", "pt_ready", "pv_done", "o_out"))
        vb_loaded = [sem(f"vb_loaded{i}") for i in range(4)]
        os_stored = [sem(f"os_stored{i}") for i in range(2)]
        oc_loaded = [sem(f"oc_loaded{i}") for i in range(2)]
        cm_max, cm_step, cm_exp, cm_rec, cm_dve, y_turned, yt_ready = (
            sem(x) for x in ("cm_max", "cm_step", "cm_exp", "cm_rec", "cm_dve", "y_turned", "yt_ready"))
        yt_stored = [sem(f"yt_stored{i}") for i in range(2)]
        past_loaded, qb_loaded = [sem(f"past_loaded{i}") for i in range(2)], [sem(f"qb_loaded{i}") for i in range(2)]
        q_turned, q_rows_ready, q_rows_stored, sk_step, sk_prod, spread_zeroed, spread_ready, rows_out, rows_turned = (sem(x) for x in (
            "q_turned", "q_rows_ready", "q_rows_stored", "sk_step", "sk_prod", "spread_zeroed", "spread_ready", "rows_out", "rows_turned"))
        smp_loaded, smp_q_ready, past_used, new_scored, st_copied, st_turned, sm_step, sm_exp, p_turned, pt_copied, smp_y_ready, smp_stored = (
            sem(x) for x in ("smp_loaded", "smp_q_ready", "past_used", "new_scored", "st_copied", "st_turned", "sm_step",
                             "sm_exp", "p_turned", "pt_copied", "smp_y_ready", "smp_stored"))
        sp_passed, dve_passed, pool_passed, pe_passed = sem("sp_passed"), sem("dve_passed"), sem("pool_passed"), sem("pe_passed")
        c_free, cf_loaded, y_loaded = sem("c_free"), sem("cf_loaded"), sem("y_loaded")
        hbh_ready, hbl_ready, res_copied = sem("hbh_ready"), sem("hbl_ready"), sem("res_copied")
        xs_loaded = [sem(f"xs_loaded{i}") for i in range(2)]
        halo_ready, carried, ftap0, ftaps, stap, gelu_done, ffh_ready, ffl_ready = (sem(x) for x in (
            "halo_ready", "carried", "ftap0", "ftaps", "stap", "gelu_done", "ffh_ready", "ffl_ready"))
        fsq_step, fms_ready, frms_ready, frstd_ready, fhn_ready, final_ready, final_stored, gx_zeroed = (sem(x) for x in (
            "fsq_step", "fms_ready", "frms_ready", "frstd_ready", "fhn_ready", "final_ready", "final_stored", "gx_zeroed"))
        final_last = sem("final_last")
        k_stored, stored = sem("k_stored"), sem("stored")

        block = ctx.enter_context(nc.Block())

        def chunks(e, body):
            body(0, True, True)
            with e.Fori(1, CHUNKS - 1) as c:
                body(c, False, True)
            body(CHUNKS - 1, False, False)

        def cols(c):
            return bass.ds(c * C, C)

        def blk(order, k, n):
            i = 4 * k + n
            dil = (4, 16, 1)[order]
            first = SMP + (k + 4 * P * n if order == 0 else i if order == 1 else P * i)
            prev = (n > 0, False, not (isinstance(i, int) and i == 0))[order]
            return Block(order, 16 * order + i, 4 * order + k, k, n, first, dil, prev)

        def attention(e, body):
            def turn(order, k, then):
                for n in range(4):
                    body(blk(order, k, n), blk(order, k, n + 1) if n < 3 else then)

            for order in range(3):
                turn(order, 0, blk(order, 1, 0))
                with e.Fori(1, 3) as k:
                    turn(order, k, blk(order, k + 1, 0))
                turn(order, 3, blk(order + 1, 0, 0) if order < 2 else None)

        def past_products(b):
            keys = past[b.n % 2][:].rearrange("p (k c) -> p k c", k=PAST_KEYS)
            return prod[:], keys[:, 1:1 + SS], keys[:, 1 + SS:]

        def sequences_done(b):
            if b.n % 2 == 0 and b.order == 1 and not (isinstance(b.idx, int) and b.idx == 16):
                return 2 * b.k + b.n // 2
            return NS if isinstance(b.idx, int) and b.idx == 32 else None

        def softmax_of(b):
            return None if b.n or not isinstance(b.k, int) else {(0, 3): 0, (1, 0): 1}.get((b.order, b.k))

        def ahead_by(cur, nxt, t, lag):
            return (cur, t + lag) if t + lag < 4 else (nxt, t + lag - 4)

        def tile_c(c, t):
            return N_A + W_OUT + (W_FFN + W_OUT + W_DOWN) * c + t

        def tile_out(c):
            return N_A if isinstance(c, int) and c == 0 else tile_c(c - 1, W_FFN)

        EV_C = (N_A + W_OUT) // 4
        EV_CHUNK = (W_FFN + W_OUT + KD) // 4

        def ev_ffn(c):
            return EV_C + EV_CHUNK * c

        def ev_out(c):
            return N_A // 4 if isinstance(c, int) and c == 0 else ev_ffn(c - 1) + W_FFN // 4

        def ev_down(c, more):
            return ev_ffn(c) + (W_FFN + (W_OUT if more else 0)) // 4

        def norm_in(c):
            return 0 if isinstance(c, int) and c == 0 else 2 * c - 1

        def norm_out(c, more):
            return 2 * c + 2 if more else 2 * c + 1

        @block.sync
        def _(e):
            def load_tile(n, s, t):
                if not (isinstance(n, int) and n < STAGE):
                    e.wait_ge(lo_ready, n - STAGE + 1)
                e.dma_start(stage[s][:], a["w"][bass.ds(t, 1)].rearrange("a p k n -> (a p) k n")).then_inc(w_loaded[s], 16)

            for k in range(KD):
                e.dma_start(xT[:, k], a["x"][:, k, 0:C]).then_inc(x0_loaded[k], 16)
            e.dma_start(gains[:], a["gains"]).then_inc(gains_loaded, 16)
            for n in range(STAGE):
                load_tile(n, n, T_IN + n)
            e.dma_start(lru_v[:], a["lru_v"]).then_inc(par_loaded, 16)
            e.dma_start(sx[:, :, :, 0:HA], a["state_a"]).then_inc(par_loaded, 16)
            e.dma_start(h0[:], a["h0"]).then_inc(par_loaded, 16)
            e.wait_ge(gw_zeroed, 1)
            for g in range(2):
                for half in range(2):
                    q = slice(64 * half, 64 * half + 64)
                    e.dma_start(gw[q, g, :, q], a["gates_w"][g, half]).then_inc(gw_loaded, 16)

            def chunk(c, first, more):
                for t in range(STAGE if first else 0, W_IN):
                    load_tile(c * W_IN + t, t % STAGE, T_IN + t)

            def passed():
                e.sem_inc(sp_passed, 1)

            def load_v(b):
                e.dma_start(vb[:, b.n], o["v"][bass.ds(b.first, P, b.dil), :]).then_inc(vb_loaded[b.n], 16)

            def load_past(b):
                e.dma_start(past[b.n % 2][:], a["past"][bass.ds(b.idx, 1)].rearrange("a p k -> (a p) k")).then_inc(past_loaded[b.n % 2], 16)
                if b.order == 0:
                    q = a["q_rows"][bass.ds(2 * b.idx - 2 * (b.n % 2), SS), D_ATT // 2 * (b.n % 2):D_ATT // 2 * (b.n % 2 + 1)]
                    e.dma_start(qb[b.n % 2][:], q.rearrange("(o s) c -> o s c", o=1).broadcast_to([P, SS, D_ATT // 2])).then_inc(qb_loaded[b.n % 2], 16)

            def attention_loads():
                load_v(blk(0, 0, 1))
                e.wait_ge(a_done, 1)
                e.dma_start(v_new[:], o["v"][0:SMP, :]).then_inc(smp_loaded, 16)
                e.dma_start(past_mask[:], a["past_mask"]).then_inc(smp_loaded, 16)
                e.dma_start(new_mask[:], a["new_mask"]).then_inc(smp_loaded, 16)
                e.wait_ge(q_rows_stored, 16)
                load_past(blk(0, 0, 0))

                def body(cur, nxt):
                    par = cur.n % 2
                    if nxt and not (isinstance(cur.idx, int) and cur.idx == 0):
                        e.wait_ge(pv_done, 4 * cur.idx)
                        passed()
                        load_v(nxt)
                    if nxt and nxt.order < 2:
                        if not (isinstance(cur.idx, int) and cur.idx == 0):
                            e.wait_ge(past_used, cur.idx)
                        passed()
                        load_past(nxt)
                    if cur.order < 2:
                        e.wait_ge(o_out, cur.idx + 1)
                        passed()
                        e.dma_start(a["os"][cur.order, bass.ds(cur.first - SMP, P, cur.dil), :], ob[par][:]).then_inc(os_stored[par], 16)
                    else:
                        y = cur.idx - 32
                        if isinstance(y, int) and y == 0:
                            for s in range(2):
                                e.wait_ge(os_stored[s], 16 * 16)
                        if not (isinstance(y, int) and y < 2):
                            e.wait_ge(cm_dve, 3 * (y - 1))
                        passed()
                        e.dma_start(oc[par][:], a["os"][:, bass.ds(cur.first - SMP, P), :].rearrange("o p n -> p o n")).then_inc(oc_loaded[par], 16)

                attention(e, body)

            chunks(e, chunk)
            for d in range(AHEAD + STAGE):
                load_tile(N_A + d, d % STAGE, T_OUT + d)
            e.wait_ge(tile_done, N_A)
            e.wait_ge(v_stored, 16 * JT * 3)
            load_v(blk(0, 0, 0))
            e.wait_ge(smp_copied, 2)
            e.dma_start(o["s_conv_a"], sx_o[:]).then_inc(stored, 16)
            e.wait_ge(smp_step, 6 * JT)
            e.dma_start(o["s_lru_h"], hs_o[:]).then_inc(stored, 16)
            e.wait_ge(smp_copied, 3)
            e.dma_start(o["p_conv_a"], xe_o[:]).then_inc(stored, 16)
            e.wait_ge(h_carried, JT * CHUNKS)
            e.dma_start(o["p_lru_h"], h_car[:]).then_inc(stored, 16)
            e.wait_ge(v_stored, 16 * JT * CHUNKS)
            attention_loads()
            e.wait_ge(k_stored, 16 * CHUNKS)
            for s in range(2):
                e.wait_ge(ya_stored[s], 16 * 2 * CHUNKS)
                e.wait_ge(yt_stored[s], 32)

            def load_y(c):
                e.dma_start(x1[:, 0:JT], a["ya"][:, :, cols(c)]).then_inc(y_loaded, 16)
                e.dma_start(x1[:, JT:], a["yb"][:, :, cols(c)]).then_inc(y_loaded, 16)

            e.wait_ge(q_copied, 48)
            e.wait_ge(smp_stored, 16)
            load_y(0)
            e.wait_ge(qk_done, 4 * 48)
            e.dma_start(cf[:], a["conv_f"]).then_inc(cf_loaded, 16)
            e.dma_start(sf[:], a["state_f"]).then_inc(cf_loaded, 16)
            for d in range(AHEAD + STAGE, W_OUT):
                load_tile(N_A + d, d % STAGE, T_OUT + d)
            for s in range(2):
                e.wait_ge(yt_stored[s], 16 * 8)

            def ffn_chunk(c, first, more):
                for t in range(W_FFN):
                    load_tile(tile_c(c, t), t % STAGE, T_FFN + t)
                    if t == 44 and more:
                        e.wait_ge(res_copied, KD * (c + 1))
                        passed()
                        load_y(c + 1)
                for d in range(W_OUT if more else 0):
                    load_tile(tile_c(c, W_FFN + d), d % STAGE, T_OUT + d)
                for s in range(W_DOWN):
                    load_tile(tile_c(c, W_FFN + (W_OUT if more else 0) + s), s % STAGE, T_DOWN + s)

            chunks(e, ffn_chunk)
            e.wait_ge(carried, FT * CHUNKS)
            e.dma_start(o["p_conv_f"], carry[:]).then_inc(stored, 16)
            e.dma_start(o["s_conv_f"], sf[:]).then_inc(stored, 16)
            e.wait_ge(stored, 16 * 6)
            e.wait_ge(final_stored, 16 * (CHUNKS - 1))

        @block.scalar
        def _(e):
            def split_hi(n, s):
                e.wait_ge(w_loaded[s % STAGE], 16 * (n // STAGE) + 16 if isinstance(n, int) else 16 // STAGE * (n - s % STAGE) + 16)
                if not (isinstance(n, int) and n < RING):
                    e.wait_ge(tile_done, n - RING + 1)
                e.activation(w_hi[s][:], stage[s % STAGE][:], ACT.Copy).then_inc(hi_ready, 1)

            for k in range(KD):
                e.wait_ge(x0_loaded[k], 16)
                e.activation(squares0[k][:], xT[:, k], ACT.Square).then_inc(sq0_ready, 1)
            split_hi(0, 0)
            e.wait_ge(ms_ready, 1)
            e.wait_ge(par_ready, 1)
            e.activation(rstd[:], bank[4][:, 0:C], ACT.Sqrt, bias=eps[:, 0:1]).then_inc(rms_ready, 1)

            def normed_hi_a(c, ks):
                for k in ks:
                    e.wait_ge(hn_ready, KD * c + k + 1)
                    e.activation(h_hi[:, k], xT[:, k], ACT.Identity, scale=gains[:, 0, k:k + 1]).then_inc(hh_ready, 1)

            e.wait_ge(gains_loaded, 16)
            normed_hi_a(0, range(4))
            split_hi(1, 1)
            normed_hi_a(0, range(4, KD))
            split_hi(2, 2)
            e.wait_ge(gw_loaded, 64)
            e.activation(gw_hi[:], gw[:], ACT.Copy).then_inc(gw_split, 1)
            e.wait_ge(par_loaded, 48)
            e.activation(sp[:, 1], lru_v[:, 2], ACT.Abs).then_inc(sp_step, 1)
            e.wait_ge(sp_step, 1)
            e.activation(sp[:, 2], sp[:, 1], ACT.Exp, scale=-1.0).then_inc(sp_step, 1)

            def copy_q(b):
                for hd in range(2):
                    rows = slice(HD * hd, HD * hd + HD)
                    ins = e.activation(qp[b.n % 2][rows, :, hd, :], qT[rows, :, bass.ds(b.first, P, b.dil)], ACT.Copy)
                ins.then_inc(q_copied, 1)

            def done(c, t):
                e.wait_ge(tile_done, c * W_IN + t + 1)
                return bank[t % 4]

            def store_v(m, c, j):
                e.wait_ge(v_turned, m + 1)
                if not (isinstance(m, int) and m == 0):
                    e.wait_ge(v_stored, 16 * m)
                e.activation(v_rows[:], bank[7][0:VR, :], ACT.Copy).then_inc(v_ready, 1)
                e.wait_ge(v_ready, m + 1)
                e.dma_start(o["v"][cols(c), j * P:(j + 1) * P].rearrange("(b i) n -> i b n", i=VR),
                            v_rows[:].rearrange("i (b n) -> i b n", n=P)).then_inc(v_stored, 16)

            def ahead(c, t):
                split_hi(c * W_IN + t + AHEAD, (t + AHEAD) % RING)

            def chunk(c, first, more):
                for j in range(JT):
                    m = JT * c + j
                    lo = SMP if first else 0
                    x_a, g_a, qk, v_t = 5 * j, 5 * j + 1, (5 * j + 2, 5 * j + 3), 5 * j + 4
                    ahead(c, x_a)
                    if not first:
                        e.wait_ge(taps, 3 * (m - JT) + 3)
                        e.activation(xe[j][:, 0:HA], xe[j][:, C:C + HA], ACT.Copy).then_inc(xa_carried, 1)
                        e.wait_ge(xa_carried, m - JT + 1)
                    elif j == 0:
                        e.wait_ge(par_ready, 1)
                    b = done(c, x_a)
                    if first:
                        e.activation(sx[:, j, :, HA:], b[:, 0:SMP].rearrange("p (n s) -> p n s", s=SS), ACT.Copy)
                    e.activation(xe[j][:, HA + lo:], b[:, lo:C], ACT.Copy).then_inc(evacuated[x_a % 4], 1)
                    e.wait_ge(evacuated[x_a % 4], 5 * c + x_a // 4 + 1)
                    if not (first and j < 2):
                        e.wait_ge(u1_ready, m - 1)
                    if first:
                        e.activation(xc[j % 2][:, 0:SMP].rearrange("p (n s) -> p n s", s=SS), sx[:, j, :, 0:SS], ACT.Identity,
                                     bias=lru_v[:, 3, j:j + 1], scale=lru_v[:, 4, j:j + 1])
                    e.activation(xc[j % 2][:, lo:], xe[j][:, lo:C], ACT.Identity,
                                 bias=lru_v[:, 3, j:j + 1], scale=lru_v[:, 4, j:j + 1]).then_inc(tap0_done, 1)
                    if j == 0 and more:
                        e.wait_ge(hl_ready, KD * (c + 1))
                        e.dma_start(xT[:], a["x"][:, :, cols(c + 1)]).then_inc(xt_loaded, 16)
                    if j == 0:
                        if not first:
                            e.wait_ge(roped, 8 * c)
                        e.dma_start(rope[:], a["rope"][:, :, cols(c)]).then_inc(rope_loaded, 16)
                    if not (first and j == 0):
                        store_v(m - 1, c if j else c - 1, (j - 1) % JT)
                    ahead(c, g_a)
                    e.wait_ge(taps, 3 * m + 3)
                    if first:
                        e.wait_ge(smp_tap, 3 * m + 3)
                    if not (first and j == 0):
                        e.wait_ge(gates_done, m)
                    e.activation(xc_hi[:], xc[j % 2][:], ACT.Copy).then_inc(xch_ready, 1)
                    b = done(c, g_a)
                    if not (first and j < 2):
                        e.wait_ge(ya_ready, m - 1)
                    e.activation(gl[j % 2][:], b[:, 0:C], ACT.Gelu_apprx_tanh).then_inc(evacuated[g_a % 4], 1)
                    if j == 2 and more:
                        e.wait_ge(ms_ready, c + 2)
                        e.wait_ge(hn_ready, KD * (c + 1))
                        e.activation(rstd[:], bank[4][:, 0:C], ACT.Sqrt, bias=eps[:, 0:1]).then_inc(rms_ready, 1)
                    for i, t in enumerate(qk):
                        ahead(c, t)
                        if i == 1:
                            e.wait_ge(gates_done, m + 1)
                            if not (first and j == 0):
                                e.wait_ge(h_carried, m)
                                e.wait_ge(ya_ready, m)
                            e.activation(r_[:], bank[5][:, 0:C], ACT.Sigmoid, bias=lru_v[:, 0, j:j + 1]).then_inc(r_ready, 1)
                            e.activation(gi[:], bank[6][:, 0:C], ACT.Sigmoid, bias=lru_v[:, 1, j:j + 1]).then_inc(gi_ready, 1)
                            e.wait_ge(r_ready, m + 1)
                            if first and j == 0:
                                e.wait_ge(sp_step, SOFTPLUS_STEPS)
                            e.activation(r_[:], r_[:], ACT.Tanh, scale=sp[:, 0, j:j + 1]).then_inc(t_ready, 1)
                        b = done(c, t)
                        if not (first and j == 0):
                            e.wait_ge(shuffled, 2 * m + i - 1)
                        e.activation(raw[i][:], b[:, 0:C], ACT.Copy).then_inc(evacuated[t % 4], 1)
                    ahead(c, v_t)
                    e.wait_ge(d1_ready, m + 1)
                    e.activation(r_[:], r_[:], ACT.Sqrt, scale=4.0).then_inc(s_ready, 1)
                    if not more and j == 3:
                        e.wait_ge(qp_zeroed, 2)
                        e.wait_ge(roped, 8 * 2)
                        copy_q(blk(0, 0, 0))
                    b = done(c, v_t)
                    if j == 3 and more:
                        normed_hi_a(c + 1, range(3))
                    if not (first and j == 0):
                        e.wait_ge(v_turned, m)
                    e.activation(v_cols[:], b[:, 0:C], ACT.Copy).then_inc(evacuated[v_t % 4], 1)
                    if j == 3 and more:
                        normed_hi_a(c + 1, range(3, KD))

            chunks(e, chunk)
            store_v(JT * CHUNKS - 1, CHUNKS - 1, JT - 1)

            def exps(b, t):
                e.wait_ge(masked, 4 * b.idx + t + 1)
                for hd in range(2):
                    v = pm[t][:, hd, (0 if b.prev else P):]
                    ins = e.activation(v, v, ACT.Exp, bias=nm[:, t, hd:hd + 1], scale=SCALE,
                                       accum_out=st[:, b.n, 1, 2 * t + hd:2 * t + hd + 1])
                ins.then_inc(exp_done, 1)

            def turned(b, t):
                u = 4 * b.idx + t
                e.wait_ge(tr_done, u + 1)
                if not (isinstance(u, int) and u < 2):
                    e.wait_ge(pv_done, u - 1)
                k0 = 0 if b.prev else 1
                e.activation(pt[t % 2][:, :, k0:], bank[4 + t % 2][:].rearrange("p (h k q) -> p h k q", h=2, k=2)[:, :, k0:],
                             ACT.Copy).then_inc(pt_ready, 1)

            def y_out(y, par):
                e.wait_ge(y_turned, y + 1)
                if not (isinstance(y, int) and y < 2):
                    e.wait_ge(yt_stored[par], 8 * (y - par))
                e.activation(yt[par][:], bank[7][:].rearrange("p (j q) -> p j q", q=P), ACT.Copy).then_inc(yt_ready, 1)
                e.wait_ge(yt_ready, y + 1)
                e.dma_start(a["yb"][:, :, bass.ds(SMP + P * y, P)], yt[par][:]).then_inc(yt_stored[par], 16)

            def combine_exp(y):
                e.wait_ge(cm_step, 11 * y + 3)
                e.activation(ce[:], ce[:], ACT.Exp, scale=SCALE).then_inc(cm_exp, 1)

            def body(cur, nxt):
                y = cur.idx - 32
                if nxt:
                    if isinstance(cur.idx, int) and cur.idx == 0:
                        e.wait_ge(roped, 8 * CHUNKS)
                    else:
                        e.wait_ge(qk_done, 4 * cur.idx)
                    copy_q(nxt)
                for t in range(4):
                    b, i = ahead_by(cur, nxt, t, 2)
                    if b:
                        exps(b, i)
                    b, i = ahead_by(cur, nxt, t, 1)
                    if b:
                        turned(b, i)
                    if softmax_of(cur) is not None:
                        sample_step(softmax_of(cur), t)
                    if sequences_done(cur) is not None:
                        sample_out(sequences_done(cur), t)
                    if cur.order == 2 and not (isinstance(y, int) and y < 1) and t == 0:
                        combine_exp(y - 1)
                    if cur.order == 2 and not (isinstance(y, int) and y < 2) and t == 1:
                        y_out(y - 2, cur.n % 2)
                if isinstance(cur.idx, int) and cur.idx == 32:
                    e.wait_ge(smp_y_ready, NS)
                    e.dma_start(a["yb"][:, :, 0:SMP], smp_y[:]).then_inc(smp_stored, 16)

            def sample_step(g, t):
                mine = slice(P * g, P * g + P)
                if t == 0:
                    e.wait_ge(new_scored, g + 1)
                    e.activation(turned_s[0:SMP, 3, mine], bank[7][0:SMP, 3 * P:], ACT.Copy).then_inc(st_copied, 1)
                if t == 2:
                    e.wait_ge(sm_step, 8 * g + 4)
                    e.activation(smp_p[:], smp_p[:], ACT.Exp, bias=smp_m[:, 2:3], scale=SCALE, accum_out=smp_m[:, 3:4]).then_inc(sm_exp, 1)
                if t == 3:
                    e.wait_ge(p_turned, g + 1)
                    e.activation(turned_s[:, 0:3, mine], bank[7][:, 0:3 * P].rearrange("p (k c) -> p k c", k=3), ACT.Copy)
                    e.activation(turned_s[0:SMP, 3, mine], bank[7][0:SMP, 3 * P:], ACT.Copy).then_inc(pt_copied, 1)

            def sample_out(done, t):
                if t == 0:
                    e.wait_ge(past_used, 2 * done + 16)
                    e.activation(out_rows[:], bank[7][0:SMP, :], ACT.Copy).then_inc(rows_out, 1)
                if t == 2:
                    e.wait_ge(rows_turned, done)
                    for hd in range(2):
                        rows = slice(HD * hd, HD * hd + HD)
                        own = bank[7][rows, 0:JT * 34].rearrange("p (t x) -> p t x", t=JT)[:, :, hd:hd + 8 * SS - 7:8]
                        ins = e.activation(smp_y[rows, :, bass.ds(SS * done - SS, SS)], own, ACT.Copy)
                    ins.then_inc(smp_y_ready, 1)

            e.wait_ge(q_turned, 1)
            e.activation(q_rows[:], bank[7][0:SMP, :], ACT.Copy).then_inc(q_rows_ready, 1)
            e.wait_ge(q_rows_ready, 1)
            e.dma_start(a["q_rows"], q_rows[:]).then_inc(q_rows_stored, 16)
            exps(blk(0, 0, 0), 0)
            exps(blk(0, 0, 0), 1)
            turned(blk(0, 0, 0), 0)
            attention(e, body)
            def ahead_c(n, t):
                split_hi(n + t + AHEAD, (t + AHEAD) % RING)

            def part_hi(g, k, src):
                e.activation(hb_hi[:, k], src, ACT.Copy).then_inc(hbh_ready, 1)

            def load_x(c, d):
                e.dma_start(xs[d % 2][:], a["x"][:, d, cols(c)]).then_inc(xs_loaded[d % 2], 16)

            def root(q):
                e.wait_ge(fms_ready, q + 1)
                e.activation(rstd[:], bank[4][:, 0:C], ACT.Sqrt, bias=eps[:, 0:1]).then_inc(frms_ready, 1)

            def heads_product(c, between=None):
                e.wait_ge(tile_done, tile_out(c))
                for k in range(KD):
                    if k == 0:
                        e.wait_ge(y_loaded, 32 * c + 32)
                    part_hi(2 * c, k, x1[:, k])
                for d in range(W_OUT):
                    if between:
                        between(d)
                    ahead_c(tile_out(c), d)
                    if d >= 1 and d + 1 < W_OUT:
                        e.wait_ge(evacuated[(d - 1) % 4], ev_out(c) + (d - 1) // 4 + 1)
                        load_x(c, d + 1)

            def store_out(c):
                e.wait_ge(final_ready, KD * (c + 1))
                e.dma_start(o["y"][:, :, cols(c)], res[:]).then_inc(final_stored, 16)

            def normed_hi(c, k):
                e.wait_ge(fhn_ready, KD * c + k + 1)
                part_hi(2 * c + 1, k, uc[k % 2][:])

            def ffn_chunk(c, first, more):
                n = tile_c(c, 0)
                for t in range(W_FFN):
                    f = t // 2
                    F = FT * c + f
                    u = f % 2
                    lo = SMP if first else 0
                    ahead_c(n, t)
                    if t == 2 and not first:
                        e.wait_ge(fhn_ready, KD * (c + 1))
                        root(2 * c)
                    if t == 12 and not first:
                        store_out(c - 1)
                    if t == 44 and more:
                        e.wait_ge(evacuated[2], ev_ffn(c))
                        e.wait_ge(evacuated[3], ev_ffn(c))
                        load_x(c + 1, 0)
                        load_x(c + 1, 1)
                    if t % 2 == 0:
                        if f > 0:
                            e.wait_ge(evacuated[(t - 1) % 4], ev_ffn(c) + (t - 1) // 4 + 1)
                            e.activation(ff_hi[:, f - 1], uc[1 - u][:], ACT.Copy).then_inc(ffh_ready, 1)
                        e.wait_ge(tile_done, n + t + 1)
                        if not (first and f < 2):
                            e.wait_ge(ftaps, 2 * F - 2)
                            e.wait_ge(carried, F - 1)
                        b = bank[t % 4]
                        if first:
                            e.activation(gs[u][:, :, HF:], b[:, 0:SMP].rearrange("p (n s) -> p n s", s=SS), ACT.Copy)
                        e.activation(gx[u][:, HF + lo:], b[:, lo:C], ACT.Copy).then_inc(evacuated[t % 4], 1)
                        e.wait_ge(evacuated[t % 4], ev_ffn(c) + t // 4 + 1)
                        e.wait_ge(halo_ready, F + 1)
                        if not (first and f < 2):
                            e.wait_ge(ffl_ready, F - 1)
                        if first:
                            e.activation(uc[u][:, 0:SMP].rearrange("p (n s) -> p n s", s=SS), gs[u][:, :, 0:SS], ACT.Identity,
                                         bias=cf[:, 0, f:f + 1], scale=cf[:, 1, f:f + 1])
                        e.activation(uc[u][:, lo:], gx[u][:, lo:C], ACT.Identity,
                                     bias=cf[:, 0, f:f + 1], scale=cf[:, 1, f:f + 1]).then_inc(ftap0, 1)
                    else:
                        e.wait_ge(ftaps, 2 * F + 2)
                        if first:
                            e.wait_ge(stap, 2 * F + 2)
                        e.activation(uc[u][:], uc[u][:], ACT.Gelu_apprx_tanh).then_inc(gelu_done, 1)
                e.wait_ge(evacuated[3], ev_ffn(c) + W_FFN // 4)
                e.activation(ff_hi[:, FT - 1], uc[1][:], ACT.Copy).then_inc(ffh_ready, 1)
                if more:
                    heads_product(c + 1)
                n = tile_c(c, W_FFN + (W_OUT if more else 0))
                for s in range(W_DOWN):
                    if more or s < W_DOWN - AHEAD:
                        ahead_c(n, s)
                    if more and s == 2:
                        root(norm_in(c + 1))
                    if more and 4 <= s < 4 + KD:
                        normed_hi(c + 1, s - 4)

            def attention_end(d):
                if d == 0:
                    combine_exp(15)
                if d == 1:
                    y_out(14, 0)
                if d == 4:
                    y_out(15, 1)

            e.wait_ge(qk_done, 4 * 48)
            e.wait_ge(k_stored, 16 * CHUNKS)
            load_x(0, 0)
            load_x(0, 1)
            heads_product(0, attention_end)
            root(0)
            for k in range(KD):
                normed_hi(0, k)
            e.wait_ge(cf_loaded, 32)
            e.wait_ge(c_free, 1)
            chunks(e, ffn_chunk)
            root(norm_out(CHUNKS - 1, False))
            for k in range(KD):
                e.wait_ge(final_ready, KD * (CHUNKS - 1) + k + 1)
                e.dma_start(o["y"][:, k, cols(CHUNKS - 1)], res[:, k]).then_inc(final_last, 16)
            e.wait_ge(final_last, 16 * KD)

        @block.vector
        def _(e):
            e.memset(gw[:], 0.0).then_inc(gw_zeroed, 1)
            e.memset(ones[:], 1.0 / D)
            for j in range(JT):
                e.memset(xe[j][:, 0:HA + SMP], 0.0)
            e.memset(a5[:], 0.0)
            e.memset(eps[:], EPS).then_inc(par_ready, 1)

            def split_lo(n, s):
                e.wait_ge(hi_ready, n + 1)
                e.tensor_tensor(w_lo[s][:], stage[s % STAGE][:], w_hi[s][:].bitcast(F32), ALU.subtract).then_inc(lo_ready, 1)

            def ahead(c, t):
                split_lo(c * W_IN + t + AHEAD, (t + AHEAD) % RING)

            def norm_scale(ks):
                for k in ks:
                    e.tensor_tensor(xT[:, k], xT[:, k], rstd[:], ALU.mult).then_inc(hn_ready, 1)

            def normed_lo_a(c, ks):
                for k in ks:
                    e.wait_ge(hh_ready, KD * c + k + 1)
                    e.scalar_tensor_tensor(out=h_lo[:, k], in0=xT[:, k], scalar=gains[:, 0, k:k + 1], in1=h_hi[:, k].bitcast(F32),
                                           op0=ALU.mult, op1=ALU.subtract).then_inc(hl_ready, 1)

            split_lo(0, 0)
            e.wait_ge(rms_ready, 1)
            e.wait_ge(gains_loaded, 16)
            e.reciprocal(rstd[:], rstd[:]).then_inc(rstd_ready, 1)
            e.wait_ge(rstd_ready, 1)
            norm_scale(range(2))
            for k in range(KD):
                if k + 2 < KD:
                    norm_scale((k + 2,))
                normed_lo_a(0, (k,))
                if k == 3:
                    split_lo(1, 1)
            split_lo(2, 2)
            e.wait_ge(gw_split, 1)
            e.tensor_tensor(gw_lo[:], gw[:], gw_hi[:].bitcast(F32), ALU.subtract).then_inc(gw_ready, 1)

            def softplus():
                x, s, s2, acc = sp[:, 2], sp[:, 3], sp[:, 4], sp[:, 5]
                count = [2]

                def step(ins):
                    ins.then_inc(sp_step, 1)
                    count[0] += 1
                    e.wait_ge(sp_step, count[0])

                e.wait_ge(sp_step, 2)
                step(e.tensor_scalar(s, x, 2.0, None, ALU.add))
                step(e.reciprocal(s, s))
                step(e.tensor_tensor(s, s, x, ALU.mult))
                step(e.tensor_tensor(s2, s, s, ALU.mult))
                step(e.memset(acc, 1.0 / 17))
                for k in range(15, 0, -2):
                    step(e.tensor_tensor(acc, acc, s2, ALU.mult))
                    step(e.tensor_scalar(acc, acc, 1.0 / k, None, ALU.add))
                step(e.tensor_tensor(acc, acc, s, ALU.mult))
                step(e.tensor_scalar(sp[:, 6], lru_v[:, 2], -1.0, 0.0, ALU.mult, ALU.max))
                step(e.tensor_scalar(acc, acc, LRU_C, None, ALU.mult))
                step(e.tensor_scalar(sp[:, 6], sp[:, 6], LRU_C / 2, None, ALU.mult))
                step(e.tensor_tensor(sp[:, 7], acc, sp[:, 6], ALU.add))
                step(e.tensor_copy(sp[:, 0], sp[:, 7]))

            def chunk(c, first, more):
                for j in range(JT):
                    m = JT * c + j
                    lo = SMP if first else 0
                    x_a, g_a, qk, v_t = 5 * j, 5 * j + 1, (5 * j + 2, 5 * j + 3), 5 * j + 4
                    ahead(c, x_a)
                    e.wait_ge(tap0_done, m + 1)
                    for i in range(1, CONV_A):
                        if first:
                            v = xc[j % 2][:, 0:SMP].rearrange("p (n s) -> p n s", s=SS)
                            if i > 1:
                                e.wait_ge(smp_tap, 3 * m + i - 1)
                            e.scalar_tensor_tensor(out=v, in0=sx[:, j, :, i:i + SS], scalar=lru_v[:, 4 + i, j:j + 1], in1=v,
                                                   op0=ALU.mult, op1=ALU.add).then_inc(smp_tap, 1)
                        if i > 1:
                            e.wait_ge(taps, 3 * m + i - 1)
                        e.scalar_tensor_tensor(out=xc[j % 2][:, lo:], in0=xe[j][:, lo + i:C + i], scalar=lru_v[:, 4 + i, j:j + 1],
                                               in1=xc[j % 2][:, lo:], op0=ALU.mult, op1=ALU.add).then_inc(taps, 1)
                    ahead(c, g_a)
                    e.wait_ge(xch_ready, m + 1)
                    e.tensor_tensor(xc_lo[:], xc[j % 2][:], xc_hi[:].bitcast(F32), ALU.subtract).then_inc(xcl_ready, 1)
                    if first and j == 0:
                        softplus()
                    for i, t in enumerate(qk):
                        ahead(c, t)
                        if not (first and j == 0):
                            e.wait_ge(roped, 2 * m + i - 1)
                        e.wait_ge(rope_loaded, 16 * c + 16)
                        e.wait_ge(evacuated[t % 4], 5 * c + t // 4 + 1)
                        q = 2 * j + i
                        e.tensor_tensor((qT if q < JT else kT)[:, q % JT, cols(c)], raw[i][:], rope[:, 0], ALU.mult)
                        e.stream_shuffle(sh[i][:], raw[i][:], SWAP).then_inc(shuffled, 1)
                        if i == 1:
                            e.wait_ge(t_ready, m + 1)
                            if not (first and j < 2):
                                e.wait_ge(ya_stored[j % 2], 32 * c + 16 * (j // 2))
                            e.tensor_scalar(d_[j % 2][:], r_[:], 1.0, None, ALU.add).then_inc(d1_ready, 1)
                            e.wait_ge(d1_ready, m + 1)
                            e.reciprocal(d_[j % 2][:], d_[j % 2][:]).then_inc(d_ready, 1)
                            e.wait_ge(d_ready, m + 1)
                            e.tensor_scalar(a_[:], d_[j % 2][:], 2.0, -1.0, ALU.mult, ALU.add).then_inc(lru_a, 1)
                        if i == 0 and j == 2 and more:
                            e.wait_ge(rms_ready, c + 2)
                            e.reciprocal(rstd[:], rstd[:]).then_inc(rstd_ready, 1)
                    if j == 3 and more:
                        normed_lo_a(c + 1, range(2))
                    ahead(c, v_t)
                    if j == 3 and more:
                        normed_lo_a(c + 1, range(2, KD))
                    e.wait_ge(u_ready, m + 1)
                    e.wait_ge(lru_a, m + 1)
                    if first:
                        v = lambda x: x[:, 0:SMP].rearrange("p (n s) -> p n s", s=SS)
                        flat = lambda x: x[:].rearrange("p n s -> p (n s)")
                        e.tensor_copy(a5[:, :, 1:], v(a_)).then_inc(smp_step, 1)
                        e.tensor_copy(u5[:, :, 1:], v(gi)).then_inc(smp_step, 1)
                        e.tensor_copy(u5[:, :, 0], h0[:, j]).then_inc(smp_step, 1)
                        e.wait_ge(smp_step, 6 * j + 3)
                        e.tensor_tensor_scan(flat(h5), flat(a5), flat(u5), 0.0, ALU.mult, ALU.add).then_inc(smp_step, 1)
                        e.wait_ge(smp_step, 6 * j + 4)
                        e.tensor_copy(v(r_), h5[:, :, 1:]).then_inc(smp_step, 1)
                        e.tensor_copy(hs_o[:, j], h5[:, :, SS]).then_inc(smp_step, 1)
                        e.wait_ge(smp_step, 6 * j + 6)
                        e.tensor_tensor_scan(r_[:, SMP:], a_[:, SMP:], gi[:, SMP:], 0.0, ALU.mult, ALU.add).then_inc(h_ready, 1)
                    else:
                        e.wait_ge(h_carried, m - JT + 1)
                        e.tensor_tensor_scan(r_[:], a_[:], gi[:], h_car[:, j:j + 1], ALU.mult, ALU.add).then_inc(h_ready, 1)
                    e.wait_ge(h_ready, m + 1)
                    e.tensor_copy(h_car[:, j:j + 1], r_[:, C - 1:C]).then_inc(h_carried, 1)

            chunks(e, chunk)

            e.wait_ge(band_ready, 1)

            def mask_max(b, t):
                u = 4 * b.idx + t
                e.wait_ge(qk_done, u + 1)
                if not (isinstance(u, int) and u < 4):
                    e.wait_ge(tr_done, u - 3)
                if t == 0 and b.order == 2 and not (isinstance(b.idx, int) and b.idx < 36):
                    e.wait_ge(cm_step, 11 * (b.idx - 35))
                k0 = 0 if b.prev else P
                e.sem_inc(dve_passed, 1)
                for hd in range(2):
                    ins = e.tensor_tensor_reduce(pm[t][:, hd, k0:], bank[t][:, 2 * P * hd + k0:2 * P * (hd + 1)], band[:, k0:],
                                                 1.0, NEG, ALU.add, ALU.max, st[:, b.n, 0, 2 * t + hd:2 * t + hd + 1])
                ins.then_inc(maxed, 1)
                e.wait_ge(maxed, u + 1)
                e.tensor_scalar(nm[:, t], st[:, b.n, 0, 2 * t:2 * t + 2], -SCALE, None, ALU.mult).then_inc(masked, 1)

            def wide(w):
                return w.rearrange("p (h o) -> p h o", o=1).broadcast_to([P, HEADS, HD])

            def heads(x):
                return x.rearrange("p (h d) -> p h d", d=HD)

            def combine_max(y, n):
                e.wait_ge(oc_loaded[n % 2], 8 * (y - n % 2) + 16)
                if not (isinstance(y, int) and y == 0):
                    e.wait_ge(cm_step, 11 * y)
                e.tensor_tensor(cm[:], oc[n % 2][:, 0, D_ATT:D_ATT + HEADS], oc[n % 2][:, 1, D_ATT:D_ATT + HEADS], ALU.max).then_inc(cm_max, 1)
                e.wait_ge(cm_max, 2 * y + 1)
                e.tensor_tensor(cm[:], cm[:], st[:, n, 0], ALU.max).then_inc(cm_max, 1)

            def combine_rec(y):
                e.wait_ge(cm_step, 11 * y + 8)
                e.reciprocal(cd[:], cd[:]).then_inc(cm_rec, 1)

            def combine_scale(y, par):
                e.wait_ge(cm_step, 11 * y + 9)
                e.tensor_tensor(heads(oc[par][:, 1, 0:D_ATT]), heads(oc[par][:, 1, 0:D_ATT]), wide(ce[:, 1]), ALU.mult).then_inc(cm_dve, 1)
                e.tensor_tensor(heads(ob[par][:, 0:D_ATT]), heads(ob[par][:, 0:D_ATT]), wide(ce[:, 2]), ALU.mult).then_inc(cm_dve, 1)

            def combine_add(y, par):
                e.wait_ge(cm_step, 11 * y + 11)
                e.tensor_tensor(ob[par][:, 0:D_ATT], ob[par][:, 0:D_ATT], oc[par][:, 1, 0:D_ATT], ALU.add).then_inc(cm_dve, 1)

            def sample_keys(b, t):
                u = b.idx
                dst = past_products(b)

                def summed(p):
                    to = turned_s[:, p, bass.ds(16 * u - 16 * (b.n % 2), 4 * HEADS)].rearrange("p (s h) -> p s h", h=HEADS)
                    return e.tensor_reduce(to[:, :, 4 * (b.n % 2):4 * (b.n % 2) + 4], dst[p].rearrange("p s (h d) -> p s h d", d=HD),
                                           AX.X, ALU.add)

                if t == 0:
                    e.wait_ge(past_loaded[b.n % 2], 8 * (u - b.n % 2) + 16)
                    e.wait_ge(qb_loaded[b.n % 2], 8 * (u - b.n % 2) + 16)
                    e.tensor_tensor(dst[2], dst[2], qb[b.n % 2][:], ALU.mult).then_inc(sk_step, 1)
                if t == 1:
                    e.wait_ge(sk_step, u + 1)
                    summed(2)
                    if isinstance(u, int) and u == 0:
                        for i in range(2):
                            e.memset(spread[i][:], 0.0).then_inc(spread_zeroed, 1)
                if t == 2:
                    e.wait_ge(sk_prod, 2 * u + 1)
                    summed(0)
                if t == 3:
                    e.wait_ge(sk_prod, 2 * u + 2)
                    summed(1).then_inc(past_used, 1)

            def sample_step(g, t):
                def step(ins, n):
                    ins.then_inc(sm_step, 1)
                    e.wait_ge(sm_step, 8 * g + n)

                if t == 1:
                    e.wait_ge(st_turned, g + 1)
                    e.wait_ge(smp_loaded, 48)
                    if g:
                        e.wait_ge(p_turned, g)
                    e.tensor_tensor_reduce(smp_p[:, 0:3 * P], bank[7][:, 0:3 * P], past_mask[:], 1.0, NEG, ALU.add, ALU.max,
                                           smp_m[:, 0:1]).then_inc(sm_step, 1)
                    new = bank[7][:, 3 * P:3 * P + SMP].rearrange("p (o k) -> p o k", o=1).broadcast_to([P, 3, SMP])
                    step(e.tensor_tensor_reduce(smp_p[:, 3 * P:].rearrange("p (o k) -> p o k", o=3), new, new_mask[:, g], 1.0, NEG,
                                                ALU.add, ALU.max, smp_m[:, 1:2]), 2)
                    step(e.tensor_tensor(smp_m[:, 0:1], smp_m[:, 0:1], smp_m[:, 1:2], ALU.max), 3)
                    step(e.tensor_scalar(smp_m[:, 2:3], smp_m[:, 0:1], -SCALE, None, ALU.mult), 4)
                if t == 2:
                    e.wait_ge(sm_exp, g + 1)
                    step(e.reciprocal(smp_m[:, 3:4], smp_m[:, 3:4]), 5)
                    step(e.tensor_scalar(smp_p[:], smp_p[:], smp_m[:, 3:4], None, ALU.mult), 6)
                    new = [smp_p[:, 3 * P + SMP * i:3 * P + SMP * (i + 1)] for i in range(3)]
                    step(e.tensor_tensor(new[1], new[1], new[2], ALU.add), 7)
                    e.tensor_tensor(new[0], new[0], new[1], ALU.add).then_inc(sm_step, 1)

            def spread_out(b):
                seq = 2 * b.k + b.n // 2
                to = spread[b.n // 2]
                if softmax_of(b) == 1:
                    e.wait_ge(pt_copied, 2)
                    e.wait_ge(spread_zeroed, 2)
                if not (isinstance(seq, int) and seq < 2):
                    e.wait_ge(past_used, b.idx - 2)
                mine = bass.ds(32 * seq, 32)
                e.tensor_copy(to[:, 0:32], turned_s[:, 0, mine])
                e.tensor_copy(to[:, 32:32 + 2 * SS * 40].rearrange("p (q r x) -> p q r x", q=2, r=SS)[:, :, :, 0:HEADS],
                              turned_s[:, 1:3, mine].rearrange("p q (r h) -> p q r h", r=SS))
                e.tensor_copy(to[0:SMP, 32 + 2 * SS * 40:], turned_s[0:SMP, 3, mine]).then_inc(spread_ready, 1)

            def body(cur, nxt):
                y = cur.idx - 32
                par = cur.n % 2
                again = cur.order == 2 and not (isinstance(y, int) and y < 1)
                for t in range(4):
                    b, i = ahead_by(cur, nxt, t, 3)
                    if b:
                        mask_max(b, i)
                    if softmax_of(cur) is not None:
                        sample_step(softmax_of(cur), t)
                    if cur.order == 1 and cur.n % 2 == 0 and t == 3:
                        spread_out(cur)
                    if cur.order == 0 and not (isinstance(cur.idx, int) and cur.idx == 0):
                        sample_keys(cur, t)
                    if again and t == 0:
                        combine_max(y - 1, (cur.n - 1) % 4)
                    if again and t == 1:
                        combine_rec(y - 1)
                    if again and t == 2:
                        combine_scale(y - 1, 1 - par)
                e.wait_ge(pv_done, 4 * cur.idx + 4)
                if cur.order < 2 or isinstance(y, int) and y < 2:
                    e.wait_ge(os_stored[par], 16 * (2 * cur.turn + cur.n // 2))
                else:
                    e.wait_ge(y_turned, y - 1)
                if cur.order < 2:
                    e.tensor_copy(ob[par][:, D_ATT:].rearrange("p (s h) -> p s h", s=2), st[:, cur.n])
                e.tensor_copy(ob[par][:, 0:D_ATT], bank[6][:]).then_inc(o_out, 1)
                if isinstance(cur.idx, int) and cur.idx == 0:
                    for t in range(4):
                        sample_keys(cur, t)
                if again:
                    combine_add(y - 1, 1 - par)

            for t in range(3):
                mask_max(blk(0, 0, 0), t)
            attention(e, body)
            combine_max(15, 3)

            def ahead_c(n, t):
                split_lo(n + t + AHEAD, (t + AHEAD) % RING)

            def part_lo(g, k, src):
                e.wait_ge(hbh_ready, KD * g + k + 1)
                e.tensor_tensor(hb_lo[:, k], src, hb_hi[:, k].bitcast(F32), ALU.subtract).then_inc(hbl_ready, 1)

            def rstd_of(q):
                e.wait_ge(frms_ready, q + 1)
                e.reciprocal(rstd[:], rstd[:]).then_inc(frstd_ready, 1)
                e.wait_ge(frstd_ready, q + 1)

            def heads_product(c, between=None):
                e.wait_ge(tile_done, tile_out(c))
                for k in range(KD):
                    part_lo(2 * c, k, x1[:, k])
                for d in range(W_OUT):
                    if between:
                        between(d)
                    ahead_c(tile_out(c), d)
                    e.wait_ge(tile_done, tile_out(c) + d + 1)
                    e.wait_ge(xs_loaded[d % 2], 64 * c + 16 * (d // 2) + 16)
                    e.tensor_tensor(x1[:, d], bank[d % 4][:, 0:C], xs[d % 2][:], ALU.add).then_inc(evacuated[d % 4], 1)

            def normed(c, k):
                if k >= 2:
                    e.wait_ge(hbl_ready, KD * (2 * c + 1) + k - 1)
                e.scalar_tensor_tensor(out=uc[k % 2][:], in0=x1[:, k], scalar=gains[:, 1, k:k + 1], in1=rstd[:],
                                       op0=ALU.mult, op1=ALU.mult).then_inc(fhn_ready, 1)

            def final(k):
                e.scalar_tensor_tensor(out=res[:, k], in0=res[:, k], scalar=gains[:, 2, k:k + 1], in1=rstd[:],
                                       op0=ALU.mult, op1=ALU.mult).then_inc(final_ready, 1)

            def ffn_chunk(c, first, more):
                n = tile_c(c, 0)
                for t in range(W_FFN):
                    f = t // 2
                    F = FT * c + f
                    u = f % 2
                    lo = SMP if first else 0
                    ahead_c(n, t)
                    if t % 2 == 0:
                        if f > 0:
                            e.wait_ge(ffh_ready, F)
                            e.tensor_tensor(ff_lo[:, f - 1], uc[1 - u][:], ff_hi[:, f - 1].bitcast(F32), ALU.subtract).then_inc(ffl_ready, 1)
                        e.wait_ge(ftap0, F + 1)
                        for i in range(1, CONV_F):
                            if first:
                                v = uc[u][:, 0:SMP].rearrange("p (n s) -> p n s", s=SS)
                                if i > 1:
                                    e.wait_ge(stap, 2 * F + 1)
                                e.scalar_tensor_tensor(out=v, in0=gs[u][:, :, i:i + SS], scalar=cf[:, 1 + i, f:f + 1], in1=v,
                                                       op0=ALU.mult, op1=ALU.add).then_inc(stap, 1)
                            if i > 1:
                                e.wait_ge(ftaps, 2 * F + 1)
                            e.scalar_tensor_tensor(out=uc[u][:, lo:], in0=gx[u][:, lo + i:C + i], scalar=cf[:, 1 + i, f:f + 1],
                                                   in1=uc[u][:, lo:], op0=ALU.mult, op1=ALU.add).then_inc(ftaps, 1)
                    else:
                        e.wait_ge(tile_done, n + t + 1)
                        e.wait_ge(gelu_done, F + 1)
                        e.tensor_tensor(uc[u][:], bank[t % 4][:, 0:C], uc[u][:], ALU.mult).then_inc(evacuated[t % 4], 1)
                    if t == 3 and not first:
                        rstd_of(2 * c)
                    if 4 <= t < 4 + KD and not first:
                        final(t - 4)
                e.wait_ge(ffh_ready, FT * c + FT)
                e.tensor_tensor(ff_lo[:, FT - 1], uc[1][:], ff_hi[:, FT - 1].bitcast(F32), ALU.subtract).then_inc(ffl_ready, 1)
                if more:
                    heads_product(c + 1)
                n = tile_c(c, W_FFN + (W_OUT if more else 0))
                for s in range(W_DOWN):
                    if more or s < W_DOWN - AHEAD:
                        ahead_c(n, s)
                    if more and s == 3:
                        rstd_of(norm_in(c + 1))
                    if more and 5 <= s < 5 + KD:
                        part_lo(2 * c + 3, s - 5, uc[(s - 5) % 2][:])
                    if more and 4 <= s < 4 + KD:
                        normed(c + 1, s - 4)
                    if s % 3 == 2:
                        d = s // 3
                        e.wait_ge(tile_done, n + s + 1)
                        if d == 0:
                            e.wait_ge(res_copied, KD * (c + 1))
                        e.tensor_tensor(res[:, d], bank[d % 4][:, 0:C], res[:, d], ALU.add).then_inc(evacuated[d % 4], 1)

            def attention_end(d):
                if d == 0:
                    combine_rec(15)
                if d == 1:
                    combine_scale(15, 1)
                if d == 2:
                    combine_add(15, 1)

            e.wait_ge(qk_done, 4 * 48)
            e.wait_ge(k_stored, 16 * CHUNKS)
            heads_product(0, attention_end)
            rstd_of(0)
            for k in range(KD):
                normed(0, k)
                if k > 0:
                    part_lo(1, k - 1, uc[(k - 1) % 2][:])
            part_lo(1, KD - 1, uc[1][:])
            e.wait_ge(c_free, 1)
            chunks(e, ffn_chunk)
            rstd_of(norm_out(CHUNKS - 1, False))
            for k in range(KD):
                final(k)

        @block.gpsimd
        def _(e):
            def square_sum(c, ks):
                base = (2 * KD - 1) * (c - 1)
                for k in ks:
                    if k == 0:
                        e.wait_ge(xt_loaded, 16 * c)
                        e.wait_ge(ms_ready, c)
                        e.tensor_tensor(ssq[:], xT[:, 0], xT[:, 0], ALU.mult).then_inc(sq_step, 1)
                    else:
                        if k > 1:
                            e.wait_ge(sq_step, base + 2 * k - 1)
                        e.tensor_tensor(sq[:], xT[:, k], xT[:, k], ALU.mult).then_inc(sq_step, 1)
                        e.wait_ge(sq_step, base + 2 * k)
                        e.tensor_tensor(ssq[:], ssq[:], sq[:], ALU.add).then_inc(sq_step, 1)

            def norm_scale(ks):
                for k in ks:
                    e.tensor_tensor(xT[:, k], xT[:, k], rstd[:], ALU.mult).then_inc(hn_ready, 1)

            def store_ya(c, j):
                e.dma_start(a["ya"][:, j, cols(c)], d_[j % 2][:]).then_inc(ya_stored[j % 2], 16)

            def store_k(c):
                e.dma_start(o["k"][:, :, cols(c)], kT[:, :, cols(c)]).then_inc(k_stored, 16)

            e.memset(ident[:], 0.0).then_inc(made, 1)
            e.memset(band[:], 0.0).then_inc(made, 1)
            e.wait_ge(made, 2)
            e.affine_select(out=ident[:], in_=ident[:], compare_op=ALU.not_equal, fill=1.0, base=0,
                            pattern=[[-1, P]], channel_multiplier=1).then_inc(ident_ready, 1)
            e.affine_select(out=band[:], in_=band[:], compare_op=ALU.is_ge, fill=NEG, base=0,
                            pattern=[[1, 2 * P]], channel_multiplier=-1).then_inc(made, 1)
            e.wait_ge(made, 3)
            e.affine_select(out=band[:], in_=band[:], compare_op=ALU.is_ge, fill=NEG, base=P,
                            pattern=[[-1, 2 * P]], channel_multiplier=1).then_inc(band_ready, 1)

            def chunk(c, first, more):
                for j in range(JT):
                    m = JT * c + j
                    if more and j < 2:
                        square_sum(c + 1, range(KD)[4 * j:4 * j + 4])
                    if not more and j == 2:
                        e.wait_ge(hl_ready, KD * CHUNKS)
                        for i in range(2):
                            e.memset(qp[i][:], 0.0).then_inc(qp_zeroed, 1)
                    for i in range(2):
                        q = 2 * j + i
                        if i == 0 and not (first and j == 0):
                            e.wait_ge(ya_ready, m)
                        e.wait_ge(shuffled, 2 * m + i + 1)
                        e.tensor_tensor(sh[i][:], sh[i][:], rope[:, 1], ALU.mult).then_inc(sin_done, 1)
                        if i == 0 and j > 0:
                            store_ya(c, j - 1)
                        elif i == 0 and not first:
                            store_ya(c - 1, JT - 1)
                            store_k(c - 1)
                        if i == 1:
                            e.wait_ge(gi_ready, m + 1)
                            e.tensor_tensor(gi[:], gi[:], xc[j % 2][:], ALU.mult).then_inc(u1_ready, 1)
                        dst = (qT if q < JT else kT)[:, q % JT, cols(c)]
                        e.wait_ge(sin_done, 2 * m + i + 1)
                        e.tensor_tensor(dst, dst, sh[i][:], ALU.add).then_inc(roped, 1)
                        if i == 0 and j == 3 and more:
                            norm_scale(range(4, KD))
                    e.wait_ge(s_ready, m + 1)
                    e.wait_ge(lru_a, m + 1)
                    e.tensor_tensor(d_[j % 2][:], d_[j % 2][:], r_[:], ALU.mult).then_inc(sd_ready, 1)
                    e.wait_ge(sd_ready, m + 1)
                    e.wait_ge(u1_ready, m + 1)
                    e.tensor_tensor(gi[:], gi[:], d_[j % 2][:], ALU.mult).then_inc(u_ready, 1)
                    e.wait_ge(u_ready, m + 1)
                    e.wait_ge(h_ready, m + 1)
                    e.wait_ge(evacuated[(5 * j + 1) % 4], 5 * c + (5 * j + 1) // 4 + 1)
                    e.tensor_tensor(d_[j % 2][:], r_[:], gl[j % 2][:], ALU.mult).then_inc(ya_ready, 1)
                    if j == 2 and more:
                        e.wait_ge(rstd_ready, c + 2)
                        norm_scale(range(4))
                if first:
                    e.wait_ge(smp_tap, 3 * JT)
                    e.tensor_copy(sx_o[:], sx[:, :, :, SS:]).then_inc(smp_copied, 2)

            chunks(e, chunk)
            e.wait_ge(ya_ready, JT * CHUNKS)
            store_ya(CHUNKS - 1, JT - 1)
            e.wait_ge(roped, 8 * CHUNKS)
            store_k(CHUNKS - 1)
            e.wait_ge(taps, 3 * JT * CHUNKS)
            for j in range(JT):
                ins = e.tensor_copy(xe_o[:, j], xe[j][:, C:C + HA])
            ins.then_inc(smp_copied, 1)

            e.wait_ge(ya_stored[0], 16 * 2 * CHUNKS)
            e.wait_ge(ya_stored[1], 16 * 2 * CHUNKS)
            e.wait_ge(v_stored, 16 * JT * CHUNKS)
            e.wait_ge(smp_copied, 3)
            e.wait_ge(tile_done, N_A)
            e.memset(smp_q[:], 0.0).then_inc(qp_zeroed, 1)
            e.wait_ge(qp_zeroed, 3)
            e.sem_inc(a_done, 1)

            def combine(y, n):
                par = n % 2
                base = 11 * y
                m = [oc[par][:, 0, D_ATT:D_ATT + HEADS], oc[par][:, 1, D_ATT:D_ATT + HEADS], st[:, n, 0]]
                l = [oc[par][:, 0, D_ATT + HEADS:], oc[par][:, 1, D_ATT + HEADS:], st[:, n, 1]]
                e.wait_ge(o_out, y + 33)
                e.wait_ge(oc_loaded[par], 8 * (y - par) + 16)
                e.wait_ge(cm_max, 2 * y + 2)
                if not (isinstance(y, int) and y == 0):
                    e.wait_ge(cm_dve, 3 * y)
                for p in range(3):
                    e.tensor_tensor(ce[:, p], m[p], cm[:], ALU.subtract).then_inc(cm_step, 1)
                e.wait_ge(cm_exp, y + 1)
                for p in range(3):
                    e.tensor_tensor(cw[:, p], ce[:, p], l[p], ALU.mult).then_inc(cm_step, 1)
                e.wait_ge(cm_step, base + 6)
                e.tensor_tensor(cd[:], cw[:, 0], cw[:, 1], ALU.add).then_inc(cm_step, 1)
                e.wait_ge(cm_step, base + 7)
                e.tensor_tensor(cd[:], cd[:], cw[:, 2], ALU.add).then_inc(cm_step, 1)
                e.wait_ge(cm_rec, y + 1)
                e.tensor_tensor(ce[:], ce[:], cd[:].rearrange("p (o h) -> p o h", o=1).broadcast_to([P, 3, HEADS]), ALU.mult).then_inc(cm_step, 1)
                e.wait_ge(cm_step, base + 9)
                o2 = oc[par][:, 0, 0:D_ATT]
                e.tensor_tensor(o2.rearrange("p (h d) -> p h d", d=HD), o2.rearrange("p (h d) -> p h d", d=HD),
                                ce[:, 0].rearrange("p (h o) -> p h o", o=1).broadcast_to([P, HEADS, HD]), ALU.mult).then_inc(cm_step, 1)
                e.wait_ge(cm_step, base + 10)
                e.wait_ge(cm_dve, 3 * y + 2)
                e.tensor_tensor(ob[par][:, 0:D_ATT], ob[par][:, 0:D_ATT], o2, ALU.add).then_inc(cm_step, 1)

            def body(cur, nxt):
                y = cur.idx - 32
                if cur.order == 0:
                    keys = past[cur.n % 2][:].rearrange("p (k c) -> p k c", k=PAST_KEYS)
                    dst = past_products(cur)
                    e.wait_ge(past_loaded[cur.n % 2], 8 * (cur.idx - cur.n % 2) + 16)
                    e.wait_ge(qb_loaded[cur.n % 2], 8 * (cur.idx - cur.n % 2) + 16)
                    if not (isinstance(cur.idx, int) and cur.idx == 0):
                        e.wait_ge(past_used, cur.idx)
                    e.tensor_tensor(dst[0], keys[:, 0:1].broadcast_to([P, SS, D_ATT // 2]), qb[cur.n % 2][:], ALU.mult).then_inc(sk_prod, 1)
                    e.tensor_tensor(dst[1], dst[1], qb[cur.n % 2][:], ALU.mult).then_inc(sk_prod, 1)
                if cur.order == 2 and not (isinstance(y, int) and y < 1):
                    combine(y - 1, (cur.n - 1) % 4)

            for hd in range(2):
                rows = slice(HD * hd, HD * hd + HD)
                ins = e.tensor_copy(smp_q[rows, :, :, hd], qT[rows, :, 0:SMP])
            ins.then_inc(smp_q_ready, 1)
            e.wait_ge(smp_q_ready, 1)
            attention(e, body)
            combine(15, 3)

            e.wait_ge(cm_step, 11 * 16)
            e.wait_ge(qk_done, 4 * 48)
            e.wait_ge(k_stored, 16 * CHUNKS)
            for i in range(2):
                e.memset(gx[i][:, 0:HF + SMP], 0.0).then_inc(gx_zeroed, 1)

            def square_sum_c(q, k, x, ev, count):
                base = (2 * KD - 1) * q
                e.wait_ge(evacuated[ev], count)
                if k == 0:
                    if not (isinstance(q, int) and q == 0):
                        e.wait_ge(fms_ready, q)
                    e.tensor_tensor(ssf[:], x, x, ALU.mult).then_inc(fsq_step, 1)
                else:
                    e.tensor_tensor(sqf[k % 2][:], x, x, ALU.mult).then_inc(fsq_step, 1)
                    e.wait_ge(fsq_step, base + 2 * k)
                    e.tensor_tensor(ssf[:], ssf[:], sqf[k % 2][:], ALU.add).then_inc(fsq_step, 1)

            def passed():
                e.sem_inc(pool_passed, 1)

            def halo(c, first, f):
                F = FT * c + f
                if not (first and f < 2):
                    e.wait_ge(ftaps, 2 * F - 2)
                if first:
                    if f == 0:
                        e.wait_ge(cf_loaded, 32)
                        e.wait_ge(gx_zeroed, 2)
                    else:
                        e.wait_ge(halo_ready, F)
                    passed()
                    e.tensor_copy(gs[f % 2][:, :, 0:HF], sf[:, f]).then_inc(halo_ready, 1)
                else:
                    e.wait_ge(carried, F - FT + 1)
                    passed()
                    e.tensor_copy(gx[f % 2][:, 0:HF], carry[:, f]).then_inc(halo_ready, 1)

            def ffn_chunk(c, first, more):
                halo(c, first, 0)
                for f in range(FT):
                    F = FT * c + f
                    if f + 1 < FT:
                        halo(c, first, f + 1)
                    e.wait_ge(halo_ready, F + 1)
                    e.wait_ge(evacuated[2 * f % 4], ev_ffn(c) + f // 2 + 1)
                    passed()
                    if first:
                        e.tensor_copy(sf[:, f], gs[f % 2][:, :, SS:])
                    e.tensor_copy(carry[:, f], gx[f % 2][:, C:]).then_inc(carried, 1)
                    if 8 <= f < 8 + KD:
                        k = f - 8
                        if not first and k == 0:
                            e.wait_ge(final_stored, 16 * c)
                            passed()
                        e.tensor_copy(res[:, k], x1[:, k]).then_inc(res_copied, 1)
                if more:
                    for d in range(W_OUT):
                        square_sum_c(norm_in(c + 1), d, x1[:, d], d % 4, ev_out(c + 1) + d // 4 + 1)
                for d in range(KD):
                    square_sum_c(norm_out(c, more), d, res[:, d], d % 4, ev_down(c, more) + d // 4 + 1)

            for d in range(W_OUT):
                square_sum_c(0, d, x1[:, d], d % 4, ev_out(0) + d // 4 + 1)
            e.wait_ge(y_turned, 16)
            e.wait_ge(yt_ready, 16)
            e.wait_ge(cm_dve, 48)
            e.wait_ge(smp_stored, 16)
            for i in range(2):
                e.wait_ge(yt_stored[i], 16 * 8)
            e.sem_inc(c_free, 1)
            chunks(e, ffn_chunk)

        @block.tensor
        def _(e):
            def product(out, s, k, hi, lo, start, stop):
                e.matmul(out, w_hi[s][:, k], hi, start=start, stop=False)
                e.matmul(out, w_hi[s][:, k], lo, start=False, stop=False)
                return e.matmul(out, w_lo[s][:, k], hi, start=False, stop=stop)

            def mean_square(c):
                e.wait_ge(sq_step, (2 * KD - 1) * c)
                e.wait_ge(rms_ready, c)
                e.matmul(bank[4][:, 0:C], ones[:], ssq[:], start=True, stop=True).then_inc(ms_ready, 1)

            def turn_v(m, b, n):
                e.wait_ge(evacuated[b], n)
                if not (isinstance(m, int) and m == 0):
                    e.wait_ge(v_ready, m)
                for i in range(C // VR):
                    last = e.transpose(bank[7][0:VR, i * P:(i + 1) * P], v_cols[:, i * VR:(i + 1) * VR], ident[:])
                last.then_inc(v_turned, 1)

            e.wait_ge(par_ready, 1)
            for k in range(KD):
                e.wait_ge(sq0_ready, k + 1)
                last = e.matmul(bank[4][:, 0:C], ones[:], squares0[k][:], start=k == 0, stop=k == KD - 1)
            last.then_inc(ms_ready, 1)
            e.wait_ge(ident_ready, 1)

            def chunk(c, first, more):
                for t in range(W_IN):
                    n = c * W_IN + t
                    e.wait_ge(lo_ready, n + 1)
                    if not (first and t < 4):
                        e.wait_ge(evacuated[t % 4], 5 * c + t // 4)
                    for k in range(KD):
                        if t == 0:
                            e.wait_ge(hl_ready, KD * c + k + 1)
                        last = product(bank[t % 4][:, 0:C], t % RING, k, h_hi[:, k], h_lo[:, k], k == 0, k == KD - 1)
                    last.then_inc(tile_done, 1)
                    if t % 5 == 2:
                        j = t // 5
                        m = JT * c + j
                        e.wait_ge(xcl_ready, m + 1)
                        if first and j == 0:
                            e.wait_ge(gw_ready, 1)
                        if not (first and j == 0):
                            e.wait_ge(r_ready, m)
                            e.wait_ge(gi_ready, m)
                        for g in range(2):
                            out = bank[5 + g][:, 0:C]
                            e.matmul(out, gw_hi[:, g, j], xc_hi[:], start=True, stop=False)
                            e.matmul(out, gw_hi[:, g, j], xc_lo[:], start=False, stop=False)
                            last = e.matmul(out, gw_lo[:, g, j], xc_hi[:], start=False, stop=True)
                        last.then_inc(gates_done, 1)
                    if t == 11 and more:
                        mean_square(c + 1)
                    if t % 5 == 0 and not (first and t == 0):
                        turn_v(JT * c + t // 5 - 1, *((t - 1) % 4, 5 * c + (t - 1) // 4 + 1))

            chunks(e, chunk)
            turn_v(JT * CHUNKS - 1, 3, 5 * CHUNKS)

            def scores(b, t):
                u = 4 * b.idx + t
                if t == 0:
                    e.wait_ge(q_copied, b.idx + 1)
                if not (isinstance(u, int) and u < 4):
                    e.wait_ge(masked, u - 3)
                n = 2 * P if b.prev else P
                keys = bass.ds(b.first - P * b.dil if b.prev else b.first, n, b.dil)
                for hd in range(2):
                    last = e.matmul(bank[t][:, 2 * P * (hd + 1) - n:2 * P * (hd + 1)], qp[b.n % 2][:, t, hd], kT[:, t, keys],
                                    start=True, stop=True)
                last.then_inc(qk_done, 1)

            def turn(b, t):
                u = 4 * b.idx + t
                e.wait_ge(exp_done, u + 1)
                if not (isinstance(u, int) and u < 2):
                    e.wait_ge(pt_ready, u - 1)
                for hd in range(2):
                    for kb in range(0 if b.prev else 1, 2):
                        i = 2 * hd + kb
                        last = e.transpose(bank[4 + t % 2][:, i * P:(i + 1) * P], pm[t][:, hd, kb * P:(kb + 1) * P], ident[:])
                last.then_inc(tr_done, 1)

            def values(b, t):
                u = 4 * b.idx + t
                e.wait_ge(pt_ready, u + 1)
                if t == 0:
                    e.wait_ge(vb_loaded[b.n], 16 * b.turn + 16)
                    e.wait_ge(o_out, b.idx)
                for hd in range(2):
                    h = slice((2 * t + hd) * HD, (2 * t + hd + 1) * HD)
                    if b.prev:
                        e.matmul(bank[6][:, h], pt[t % 2][:, hd, 0], vb[:, (b.n - 1) % 4, h], start=True, stop=False)
                    last = e.matmul(bank[6][:, h], pt[t % 2][:, hd, 1], vb[:, b.n, h], start=not b.prev, stop=True)
                last.then_inc(pv_done, 1)

            def turn_y(y, par):
                e.wait_ge(cm_dve, 3 * y + 3)
                if not (isinstance(y, int) and y < 1):
                    e.wait_ge(yt_ready, y)
                else:
                    e.wait_ge(smp_y_ready, NS)
                for j in range(JT):
                    last = e.transpose(bank[7][:, j * P:(j + 1) * P], ob[par][:, j * P:(j + 1) * P], ident[:])
                last.then_inc(y_turned, 1)

            def group(x):
                return x.rearrange("p (k h) -> p k h", h=HEADS)

            def sample_step(g, i):
                mine = slice(P * g, P * g + P)
                if i == 0:
                    e.wait_ge(smp_q_ready, 1)
                    if g:
                        e.wait_ge(pt_copied, g)
                    else:
                        e.wait_ge(q_rows_ready, 1)
                    for t in range(JT):
                        last = e.matmul(group(bank[7][0:SMP, 3 * P:])[:, :, 2 * t:2 * t + 2], kT[:, t, 0:SMP],
                                        smp_q[:, t, 16 * g:16 * g + 16, :], start=True, stop=True)
                    last.then_inc(new_scored, 1)
                if i == 1:
                    e.wait_ge(st_copied, g + 1)
                    e.wait_ge(past_used, 8 * g + 8)
                    for p in range(3):
                        e.transpose(bank[7][:, p * P:(p + 1) * P], turned_s[:, p, mine], ident[:])
                    e.transpose(bank[7][:, 3 * P:3 * P + SMP], turned_s[0:SMP, 3, mine], ident[0:SMP, 0:SMP]).then_inc(st_turned, 1)
                if i == 3:
                    e.wait_ge(sm_step, 8 * g + 8)
                    for p in range(3):
                        e.transpose(bank[7][:, p * P:(p + 1) * P], smp_p[:, p * P:(p + 1) * P], ident[:])
                    e.transpose(bank[7][0:SMP, 3 * P:], smp_p[:, 3 * P:3 * P + SMP], ident[:]).then_inc(p_turned, 1)

            def passed():
                e.sem_inc(pe_passed, 1)

            def sample_values(b):
                half = slice(D_ATT // 2 * (b.n % 2), D_ATT // 2 * (b.n % 2 + 1))
                probs = spread[b.n // 2]
                out = bank[7][0:SMP, half]
                values_ = past[b.n % 2][:].rearrange("p (k c) -> p k c", k=PAST_KEYS)
                if b.n % 2 == 0:
                    e.wait_ge(spread_ready, 2 * b.k + b.n // 2 + 1)
                    if sequences_done(b) is not None:
                        e.wait_ge(smp_y_ready, sequences_done(b))
                e.wait_ge(past_loaded[b.n % 2], 8 * (b.idx - b.n % 2) + 16)
                passed()
                e.matmul(out, probs[0:SMP, 32 + 2 * SS * 40:], v_new[:, half], start=True, stop=False)
                e.matmul(out, probs[:, 0:32], values_[:, 0], start=False, stop=False)
                for kb in range(2 * SS):
                    at = 32 + SS * 40 * (kb // SS) + 32 * (kb % SS)
                    last = e.matmul(out, probs[:, at:at + 32], values_[:, 1 + kb], start=False, stop=kb == 2 * SS - 1)
                last.then_inc(past_used, 1)

            def turn_rows(done, t):
                if t == 1:
                    e.wait_ge(rows_out, done)
                    passed()
                    for i in range(JT):
                        last = e.transpose(bank[7][:, SMP * i:SMP * (i + 1)], out_rows[:, P * i:P * (i + 1)], ident[0:SMP, 0:SMP])
                    last.then_inc(rows_turned, 1)

            def body(cur, nxt):
                y = cur.idx - 32
                for t in range(4):
                    if softmax_of(cur) is not None:
                        sample_step(softmax_of(cur), t)
                    if sequences_done(cur) is not None:
                        turn_rows(sequences_done(cur), t)
                    b, i = ahead_by(cur, nxt, t, 3)
                    if b:
                        scores(b, i)
                    b, i = ahead_by(cur, nxt, t, 1)
                    if b:
                        turn(b, i)
                    values(cur, t)
                    if cur.order == 2 and not (isinstance(y, int) and y < 2) and t == 0:
                        turn_y(y - 2, cur.n % 2)
                if cur.order == 1:
                    sample_values(cur)

            for i in range(4):
                e.wait_ge(evacuated[i], 5 * CHUNKS)
            e.wait_ge(rms_ready, CHUNKS)
            e.wait_ge(gi_ready, JT * CHUNKS)
            for t in range(3):
                scores(blk(0, 0, 0), t)
            e.wait_ge(v_ready, JT * CHUNKS)
            for t in range(JT):
                last = e.transpose(bank[7][0:SMP, t * P:(t + 1) * P], qT[:, t, 0:SMP], ident[:])
            last.then_inc(q_turned, 1)
            turn(blk(0, 0, 0), 0)
            attention(e, body)
            def mean_square_c(q):
                e.wait_ge(fsq_step, (2 * KD - 1) * (q + 1))
                if not (isinstance(q, int) and q == 0):
                    e.wait_ge(frms_ready, q)
                e.matmul(bank[4][:, 0:C], ones[:], ssf[:], start=True, stop=True).then_inc(fms_ready, 1)

            def dense(n, t, ev, g):
                e.wait_ge(lo_ready, n + t + 1)
                e.wait_ge(evacuated[t % 4], ev + t // 4)
                for k in range(KD):
                    if t == 0:
                        e.wait_ge(hbl_ready, KD * g + k + 1)
                    last = product(bank[t % 4][:, 0:C], t % RING, k, hb_hi[:, k], hb_lo[:, k], k == 0, k == KD - 1)
                last.then_inc(tile_done, 1)

            def ffn_chunk(c, first, more):
                for t in range(W_FFN):
                    dense(tile_c(c, 0), t, ev_ffn(c), 2 * c + 1)
                    if t == 1 and not first:
                        mean_square_c(2 * c)
                if more:
                    for d in range(W_OUT):
                        dense(tile_out(c + 1), d, ev_out(c + 1), 2 * c + 2)
                n = tile_c(c, W_FFN + (W_OUT if more else 0))
                for s in range(W_DOWN):
                    d, g = s // 3, s % 3
                    e.wait_ge(lo_ready, n + s + 1)
                    if d == 0:
                        e.wait_ge(ffl_ready, FT * c + KD * (g + 1))
                    if g == 0:
                        e.wait_ge(evacuated[d % 4], ev_down(c, more) + d // 4)
                    for k in range(KD):
                        last = product(bank[d % 4][:, 0:C], s % RING, k, ff_hi[:, KD * g + k], ff_lo[:, KD * g + k],
                                       g == 0 and k == 0, g == 2 and k == KD - 1)
                    last.then_inc(tile_done, 1)
                    if more and s == 1:
                        mean_square_c(norm_in(c + 1))

            e.wait_ge(masked, 4 * 48)
            for d in range(W_OUT):
                dense(tile_out(0), d, ev_out(0), 0)
                if d == 0:
                    turn_y(14, 0)
                if d == 3:
                    turn_y(15, 1)
            mean_square_c(0)
            chunks(e, ffn_chunk)
            mean_square_c(norm_out(CHUNKS - 1, False))


Block = namedtuple("Block", "order idx turn k n first dil prev")
SWAP = [i + 8 if i < 8 else i - 8 if i < 16 else i for i in range(32)]


def column_tiles(w):
    k, n = w.shape
    return w.reshape(k // P, P, n // P, P).transpose(2, 1, 0, 3)


def by_channel(x):
    x = np.moveaxis(x, -1, 0)
    return x.reshape((x.shape[0] // P, P) + x.shape[1:]).swapaxes(0, 1)


def rotary_tables():
    half = ROT // 2
    inv = np.float32(500000.0) ** (np.float32(-2.0) * np.arange(half, dtype=np.float32) / np.float32(ROT))
    pos = np.concatenate([np.tile(PAST + np.arange(SS), NS), np.arange(SEQ)]).astype(np.float32)
    ang = inv.astype(np.float32)[:, None] * pos[None]
    out = np.zeros((P, 2, TOK), np.float32)
    out[:, 0] = 1.0
    for h in range(P // HD):
        for i in range(2):
            rows = slice(h * HD + i * half, h * HD + (i + 1) * half)
            out[rows, 0] = np.cos(ang)
            out[rows, 1] = np.sin(ang) * (1 if i else -1)
    return out


def past_blocks(x):
    n, w, ch = x.shape
    return np.concatenate([
        x[:, None, w - P:],
        x[:, w - 4 * P:].reshape(n, P, 4, ch).swapaxes(1, 2),
        x.reshape(n, P, 16, ch)[:, :, :SS].swapaxes(1, 2)], 1)


def past_units(k, v):
    k, v = past_blocks(k), past_blocks(v)
    k, v = (x.reshape(NS, PAST_KEYS, P, 2, 2 * P).transpose(0, 3, 2, 1, 4) for x in (k, v))
    return np.concatenate([x.reshape(2 * NS, P, 2 * PAST_KEYS * P) for x in (k, v)])


def sample_masks():
    row = np.arange(P)
    seq, tok = row // 32, row // HEADS % SS
    past = np.zeros((P, 3 * P), np.float32)
    past[:, :P] = np.where(np.arange(P)[None] >= tok[:, None], 0.0, NEG)
    new = np.full((P, 2, 3, SMP), NEG, np.float32)
    key = np.arange(SMP)
    for g in range(2):
        mine = (key // SS)[None] == 4 * g + seq[:, None]
        new[:, g, 0][mine & ((key % SS)[None] <= tok[:, None])] = 0.0
        for p in (1, 2):
            new[:, g, p][mine & ((key % SS)[None] == tok[:, None])] = 0.0
    return past, new


def by_token(x):
    x = x.swapaxes(0, 1)
    return np.moveaxis(x.reshape((-1,) + x.shape[2:]), 0, -1)


def kernel(**inputs):
    import concourse.bacc as bacc
    from concourse.bass_utils import run_bass_kernel_spmd

    x = {k: np.asarray(v) for k, v in inputs.items()}
    tiles = column_tiles(x["w_in"][0])
    order = [y for j in range(JT) for y in (j, JT + j, 2 * JT + 2 * j, 2 * JT + 2 * j + 1, 4 * JT + j)]
    gate, up = column_tiles(x["w_ffn_gate"][0]), column_tiles(x["w_ffn_up"][0])
    down = x["w_ffn_down"][0].reshape(3, D, D)
    down = np.stack([column_tiles(down[g]) for g in range(3)], 1).reshape(W_DOWN, P, KD, P)
    arrays = {
        "x": by_channel(np.concatenate([x["x_sample"].reshape(SMP, D), x["x_prompt"][0]])),
        "w": np.concatenate([tiles[order], column_tiles(x["w_out"][0]), np.stack([gate, up], 1).reshape(W_FFN, P, KD, P), down]),
        "gains": by_channel(np.stack([x["g_mix"][0], x["g_ffn"][0], x["g_final"]])).swapaxes(1, 2),
        "lru_v": by_channel(np.concatenate([x["lru_b_r"], x["lru_b_i"], x["lru_lambda"], x["conv_a_b"], x["conv_a_w"][0]])).swapaxes(1, 2),
        "state_a": by_channel(x["state_conv_a"][0]),
        "h0": by_channel(x["state_lru_h"][0]),
        "gates_w": np.stack([x["lru_w_r"][0], x["lru_w_i"][0]]).reshape(2, JT, 2, HD, HD).transpose(0, 2, 3, 1, 4),
        "rope": rotary_tables(),
        "conv_f": by_channel(np.concatenate([x["conv_f_b"], x["conv_f_w"][0]])).swapaxes(1, 2),
        "state_f": by_channel(x["state_conv_ffn"][0]),
    }
    arrays["past"] = past_units(x["cache_win_k"][0].reshape(NS, -1, D_ATT), x["cache_win_v"][0].reshape(NS, -1, D_ATT))
    arrays["past_mask"], arrays["new_mask"] = sample_masks()
    outs = {
        "k": (P, JT, TOK), "v": (TOK, D_ATT), "y": (P, KD, TOK), "s_conv_a": (P, JT, NS, HA), "s_lru_h": (P, JT, NS),
        "p_conv_a": (P, JT, HA), "p_lru_h": (P, JT), "s_conv_f": (P, FT, NS, HF), "p_conv_f": (P, FT, HF),
    }
    nc = bacc.Bacc("TRN2", target_bir_lowering=False, num_devices=1)
    arrays = {k: np.ascontiguousarray(v) for k, v in arrays.items()}
    a = {k: nc.dram_tensor("in_" + k, v.shape, F32, kind="ExternalInput").ap() for k, v in arrays.items()}
    o = {k: nc.dram_tensor("out_" + k, s, F32, kind="ExternalOutput").ap() for k, s in outs.items()}
    a["os"] = nc.dram_tensor("attention_rows", (2, SEQ, OS), F32, kind="Internal").ap()
    a["ya"] = nc.dram_tensor("mixed_lru", (P, JT, TOK), F32, kind="Internal").ap()
    a["yb"] = nc.dram_tensor("mixed_attention", (P, JT, TOK), F32, kind="Internal").ap()
    a["q_rows"] = nc.dram_tensor("query_rows", (SMP, D_ATT), F32, kind="Internal").ap()
    build(nc, a, o)
    r = run_bass_kernel_spmd(nc, [{"in_" + k: v for k, v in arrays.items()}], core_ids=[0]).results[0]
    r = {k: r["out_" + k] for k in outs}
    y, k = by_token(r["y"]), by_token(r["k"])
    return (
        y[SMP:].reshape(1, SEQ, D), y[:SMP].reshape(NS, SS, D),
        by_token(r["p_conv_a"]).reshape(1, 1, HA, D_LRU), by_token(r["p_lru_h"]).reshape(1, 1, D_LRU),
        k[SMP:].reshape(1, 1, SEQ, HEADS, HD), r["v"][SMP:].reshape(1, 1, SEQ, HEADS, HD),
        by_token(r["p_conv_f"]).reshape(1, 1, HF, FF),
        by_token(r["s_conv_a"]).reshape(1, NS, HA, D_LRU), by_token(r["s_lru_h"]).reshape(1, NS, D_LRU),
        k[:SMP].reshape(1, NS, SS, HEADS, HD), r["v"][:SMP].reshape(1, NS, SS, HEADS, HD),
        by_token(r["s_conv_f"]).reshape(1, NS, HF, FF),
    )
```
